# Optimizing a Trainium2 kernel written in Bass

```python
import jax, jax.numpy as jnp
from jax import lax
import numpy as np

D_MODEL = 1024
BATCH = 1
SEQ = 512
DEPTH = 2

N_META = 16
GRID_W = 64
N_HEADS = 8
N_KV_HEADS = 2
HEAD_DIM = 128
GQA_GROUP = N_HEADS // N_KV_HEADS
ATTN_WIDTH = N_HEADS * HEAD_DIM
KV_WIDTH = N_KV_HEADS * HEAD_DIM
ROT_HALF = HEAD_DIM // 2
ROPE_THETA = 10000.0
Q_BLOCK = 128
F_GROUPS = 4
F_GROUP_DIM = 128
F_WIDTH = F_GROUPS * F_GROUP_DIM
N_BRANCH = 2
IN_WIDTH = 2 * F_WIDTH + 2 * ATTN_WIDTH + 2 * KV_WIDTH + N_BRANCH * D_MODEL
EPS = 1e-6

kernel_name = "hybrid_fnet_axialgqa_gated_encoder"

def rms_norm(x, g):
    xf = x.astype(jnp.float32)
    y = xf * lax.rsqrt(jnp.mean(xf * xf, axis=-1, keepdims=True) + EPS)
    return (y * g.astype(jnp.float32)).astype(x.dtype)

def axial_angles(n_tokens):
    rows = n_tokens // GRID_W
    r = jnp.repeat(jnp.arange(rows, dtype=jnp.float32), GRID_W)
    c = jnp.tile(jnp.arange(GRID_W, dtype=jnp.float32), rows)
    pad = jnp.zeros((N_META,), jnp.float32)
    r = jnp.concatenate([pad, r])
    c = jnp.concatenate([pad, c])
    inv_freq = ROPE_THETA ** (-jnp.arange(0, ROT_HALF, 2, dtype=jnp.float32) / ROT_HALF)
    return r[:, None] * inv_freq[None, :], c[:, None] * inv_freq[None, :]

def rope_1d(x, ang):
    x1, x2 = jnp.split(x, 2, axis=-1)
    c = jnp.cos(ang)[:, None, :].astype(x.dtype)
    s = jnp.sin(ang)[:, None, :].astype(x.dtype)
    return jnp.concatenate([x1 * c - x2 * s, x2 * c + x1 * s], axis=-1)

def axial_rope(x, ang_r, ang_c):
    return jnp.concatenate([rope_1d(x[..., :ROT_HALF], ang_r), rope_1d(x[..., ROT_HALF:], ang_c)], axis=-1)

def attend(qb, k, v):
    scale = HEAD_DIM ** -0.5
    s = jnp.einsum('bqkgd,bskd->bkgqs', qb, k).astype(jnp.float32) * scale
    p = jax.nn.softmax(s, axis=-1).astype(v.dtype)
    return jnp.einsum('bkgqs,bskd->bqkgd', p, v)

def bidirectional_gqa(q, k, v):
    b, s_tot = q.shape[0], q.shape[1]
    n_real = s_tot - N_META
    q = q.reshape(b, s_tot, N_KV_HEADS, GQA_GROUP, HEAD_DIM)
    o_meta = attend(q[:, :N_META], k, v)
    q_real = q[:, N_META:].reshape(b, n_real // Q_BLOCK, Q_BLOCK, N_KV_HEADS, GQA_GROUP, HEAD_DIM)
    q_real = jnp.transpose(q_real, (1, 0, 2, 3, 4, 5))
    o_real = lax.map(lambda qb: attend(qb, k, v), q_real)
    o_real = jnp.transpose(o_real, (1, 0, 2, 3, 4, 5)).reshape(b, n_real, N_KV_HEADS, GQA_GROUP, HEAD_DIM)
    o = jnp.concatenate([o_meta, o_real], axis=1)
    return o.reshape(b, s_tot, ATTN_WIDTH)

def fourier_mix(u, w_mix):
    b, s, _ = u.shape
    uf = u.astype(jnp.float32).reshape(b, s, F_GROUPS, F_GROUP_DIM)
    z = jnp.fft.fft2(uf, axes=(1, 3), norm='ortho').real.astype(u.dtype)
    return jnp.einsum('bsgc,gcd->bsgd', z, w_mix).reshape(b, s, F_WIDTH)

def hybrid_layer(h, g_norm, w_in, b_gate, q_g, k_g, w_fmix, w_fproj, w_aproj, w_out, ang_r, ang_c):
    b, s, _ = h.shape
    xn = rms_norm(h, g_norm)
    proj = xn @ w_in
    p1 = F_WIDTH
    p2 = p1 + F_WIDTH
    p3 = p2 + ATTN_WIDTH
    p4 = p3 + KV_WIDTH
    p5 = p4 + KV_WIDTH
    p6 = p5 + ATTN_WIDTH
    f_val, f_gate, q, k, v, a_gate, gate_logits = jnp.split(proj, [p1, p2, p3, p4, p5, p6], axis=-1)
    y_f = (fourier_mix(f_val, w_fmix) * jax.nn.silu(f_gate)) @ w_fproj
    q = axial_rope(rms_norm(q.reshape(b, s, N_HEADS, HEAD_DIM), q_g), ang_r, ang_c)
    k = axial_rope(rms_norm(k.reshape(b, s, N_KV_HEADS, HEAD_DIM), k_g), ang_r, ang_c)
    v = v.reshape(b, s, N_KV_HEADS, HEAD_DIM)
    o = bidirectional_gqa(q, k, v)
    y_a = (o * jax.nn.silu(a_gate)) @ w_aproj
    gates = jax.nn.sigmoid(gate_logits + b_gate)
    g_f, g_a = jnp.split(gates, 2, axis=-1)
    return h + (g_f * y_f + g_a * y_a) @ w_out

def setup_inputs(seed: int = 0) -> dict:
    key = jax.random.key(seed)
    ks = jax.random.split(key, 12)
    f32 = jnp.float32
    x = jax.random.normal(ks[0], (BATCH, SEQ, D_MODEL), f32)
    meta_tokens = jax.random.normal(ks[1], (N_META, D_MODEL), f32)
    norm_g = 1.0 + 0.02 * jax.random.normal(ks[2], (DEPTH, D_MODEL), f32)
    w_in = jax.random.normal(ks[3], (DEPTH, D_MODEL, IN_WIDTH), f32) * D_MODEL ** -0.5
    b_gate = 0.02 * jax.random.normal(ks[4], (DEPTH, N_BRANCH * D_MODEL), f32)
    q_norm_g = 1.0 + 0.02 * jax.random.normal(ks[5], (DEPTH, HEAD_DIM), f32)
    k_norm_g = 1.0 + 0.02 * jax.random.normal(ks[6], (DEPTH, HEAD_DIM), f32)
    w_fmix = jax.random.normal(ks[7], (DEPTH, F_GROUPS, F_GROUP_DIM, F_GROUP_DIM), f32) * F_GROUP_DIM ** -0.5
    w_fproj = jax.random.normal(ks[8], (DEPTH, F_WIDTH, D_MODEL), f32) * F_WIDTH ** -0.5
    w_aproj = jax.random.normal(ks[9], (DEPTH, ATTN_WIDTH, D_MODEL), f32) * ATTN_WIDTH ** -0.5
    w_out = jax.random.normal(ks[10], (DEPTH, D_MODEL, D_MODEL), f32) * D_MODEL ** -0.5
    return {"x": x, "meta_tokens": meta_tokens, "norm_g": norm_g, "w_in": w_in, "b_gate": b_gate,
            "q_norm_g": q_norm_g, "k_norm_g": k_norm_g, "w_fmix": w_fmix, "w_fproj": w_fproj,
            "w_aproj": w_aproj, "w_out": w_out}

def reference(x, meta_tokens, norm_g, w_in, b_gate, q_norm_g, k_norm_g, w_fmix, w_fproj, w_aproj, w_out):
    b = x.shape[0]
    meta = jnp.broadcast_to(meta_tokens[None].astype(x.dtype), (b, N_META, x.shape[2]))
    h = jnp.concatenate([meta, x], axis=1)
    ang_r, ang_c = axial_angles(x.shape[1])
    for l in range(DEPTH):
        h = hybrid_layer(h, norm_g[l], w_in[l], b_gate[l], q_norm_g[l], k_norm_g[l], w_fmix[l],
                         w_fproj[l], w_aproj[l], w_out[l], ang_r, ang_c)
    return h[:, N_META:]


_drawn_inputs = setup_inputs


def setup_inputs(seed=0):
    import zlib

    import numpy as np

    out = dict(_drawn_inputs(seed))
    spreads = {}
    factors = {'norm_g': 5.81, 'b_gate': 8.0, 'q_norm_g': 8.0, 'k_norm_g': 8.0}
    for name, (base, spread) in spreads.items():
        noise = np.random.default_rng([zlib.crc32(name.encode()), seed]).standard_normal(out[name].shape)
        drawn = base * np.exp(spread * noise) if base else spread * noise
        out[name] = __import__('jax').numpy.asarray(drawn.astype(out[name].dtype))
    for name, factor in factors.items():
        out[name] = (out[name] * factor).astype(out[name].dtype)
    return out
```

```python
from contextlib import ExitStack

import numpy as np

import concourse.bass as bass
from concourse import mybir

F32, F32R = mybir.dt.float32, mybir.dt.float32r
ALU, ACT, AX = mybir.AluOpType, mybir.ActivationFunctionType, mybir.AxisListType

P = 128
D, SEQ, DEPTH, META = 1024, 512, 2, 16
S = SEQ + META
NC = D // P
HALF = S // 2
HEADS, KV, GQA, HD = 8, 2, 4, 128
FG = 4
ROW_TILES = SEQ // P
KCH = 5
TAIL = 4 * P
NT = 88
NP_ = S // NT
EPS = 1e-6
SCALE = HD ** -0.5
QUARTER = 32
FT, FCH = 89, 3
FS = 266
FOLD = S // 2

C_FVAL, C_FGATE, C_Q, C_K, C_V = 0, 512, 1024, 2048, 2304
C_AGATE, C_GF, C_GA = 2560, 3584, 4608

T_K0, T_Q0, T_K1, T_V0, T_V1 = range(5)
T_HEAD = 5
T_AG7, T_FG0 = T_HEAD + 14, T_HEAD + 15
T_FOUR = T_HEAD + 16
T_FV3 = T_FOUR + 6
T_MIX = T_FV3 + 1
T_OUT = T_MIX + 4 * NC
TL = T_OUT + NC

U_RMS, U_K0, U_Q0, U_K1, U_V0, U_V1 = range(6)
U_HEAD = 6
U_QM = U_HEAD + 5 * 7
U_M0, U_M1, U_H7 = U_QM + 1, U_QM + 2, U_QM + 3
U_CW = U_H7 + 4
U_A = U_CW + 1
UL = U_A + FG
W_RMS, W_K0, W_K1 = range(3)
W_HEAD = 3
W_M0, W_H7 = W_HEAD + 28, W_HEAD + 30
W_F = W_H7 + 4
WL = W_F + FG
O_V0, O_V1 = range(2)
O_HEAD = 2
O_M0 = O_HEAD + 14
O_H7 = O_M0 + 4
O_SW = O_H7 + 2
O_B = O_SW + 1
OL = O_B + FG
QT_M0, QT_H7, QTL = 28, 30, 34
ROPES = 10
R_H, R_K0, R_Q0, R_K1, R_QNEXT, R_QM, RL = 0, 1, 2, 3, 4, 11, 12
Q_COL, M_COL = 8, 12
NORMS = 3
ATT = 10
A_M0, A_H7 = 7, 9
H_FG, H_MIX, HL = HEADS, HEADS + FG, HEADS + FG + 2 * NC


def program(nc, x, meta, norm_g, w_in, b_gate, q_g, k_g, w_fmix, w_fproj, w_aproj, w_out,
            eye, rope, dft_pos, dft_ch, out):
    with ExitStack() as ctx:
        def sb(name, shape, dt=F32):
            return ctx.enter_context(nc.sbuf_tensor(name, shape, dt))

        def ps(name, shape):
            return ctx.enter_context(nc.psum_tensor(name, shape, F32))

        def sem(name):
            return ctx.enter_context(nc.semaphore(name))

        h_t = sb("h_t", [P, NC, S])
        x_hi, x_lo = sb("x_hi", [P, NC, S], F32R), sb("x_lo", [P, NC, S], F32R)
        w_raw = sb("w_raw", [P, 2, NC, P])
        w_hi, w_lo = sb("w_hi", [P, 2, NC, P], F32R), sb("w_lo", [P, 2, NC, P], F32R)
        att_hi, att_lo = sb("att_hi", [P, NC, S], F32R), sb("att_lo", [P, NC, S], F32R)
        kvz = sb("kvz", [P, 4672], F32R)
        phase = sb("phase", [P, 2 * NC * S], F32R)
        arena = sb("arena", [P, 11 * S])
        rstd = sb("rstd", [P, S])
        rot = sb("rot", [P, 4, S])
        sqsum = sb("sqsum", [P, S])
        fgate = sb("fgate", [P, FG, S])
        ident = sb("ident", [P, P])
        ones = sb("ones", [P, P])
        ngain = sb("ngain", [P, DEPTH + 1, NC])
        bhalf = sb("bhalf", [P, DEPTH, 2 * NC])
        gains = sb("gains", [P, DEPTH, 4])
        ms = sb("ms", [P, 16])
        rs = sb("rs", [P, 16])
        halfneg = sb("halfneg", [P, 16])
        rmax = sb("rmax", [P, 2])
        nbias = sb("nbias", [P, 2])
        rsum = sb("rsum", [P, 2])
        rinv = sb("rinv", [P, 2])
        qm_sq = sb("qm_sq", [P, HEADS, META])
        agm = sb("agm", [P, HEADS, META])

        def region(t, at, *shape):
            n = int(np.prod(shape))
            v = t[:, at:at + n]
            if len(shape) == 2:
                v = v.rearrange("p (a b) -> p a b", a=shape[0])
            if len(shape) == 3:
                v = v.rearrange("p (a b c) -> p a b c", a=shape[0], b=shape[1])
            return v

        k_hi, k_lo = region(kvz, 0, KV, S), region(kvz, KV * S, KV, S)
        v_hi = region(kvz, 2 * KV * S, KV, KCH, P)
        v_lo = region(kvz, 2 * KV * S + KV * KCH * P, KV, KCH, P)
        z_hi, z_lo = region(kvz, 0, FG, S), region(kvz, FG * S, FG, S)
        m_hi, m_lo = region(phase, 0, NC, S), region(phase, NC * S, NC, S)
        pt_hi, pt_lo = region(phase, 0, 4, 4 * P), region(phase, 2048, 4, 4 * P)
        tail_hi, tail_lo = region(phase, 4096, 4 * P), region(phase, 4608, 4 * P)
        q_hi, q_lo = region(phase, 5120, S), region(phase, 5120 + S, S)
        qm_hi, qm_lo = region(phase, 6176, HEADS, META), region(phase, 6304, HEADS, META)
        xf_hi, xf_lo = region(phase, 0, 2, FT * FCH), region(phase, 534, 2, FT * FCH)
        pq_hi, pq_lo = region(phase, 1068, 2 * FCH, P), region(phase, 1836, 2 * FCH, P)
        cw_hi, cw_lo = region(phase, 2604, 2, FG, P), region(phase, 3628, 2, FG, P)
        ft_hi, ft_lo = region(phase, 4652, 2, FCH, FS), region(phase, 6248, 2, FCH, FS)

        def slot(n, k=1):
            return arena[:, n * S:(n + k) * S]

        prob = slot(0, 2).rearrange("p (a b) -> p a b", a=2)
        rp_raw, rp_swap, rp_sq, rp_a, rp_b = slot(2), slot(3), slot(4), slot(5), slot(6)
        ag_raw, ag_th, silu, att = slot(7), slot(8), slot(9), slot(10)
        diag = slot(10)
        v_t = slot(7, 2).rearrange("p (a b) -> p a b", a=2)
        def span(at, n):
            return arena[:, at:at + n]

        fv = slot(0)
        fold = span(S, 2 * FT * FCH).rearrange("p (a b) -> p a b", a=2)
        fb, fz = span(1062, FS), span(1328, S)
        ft_raw, ch_raw, fm_raw = span(1856, 2 * FCH * FS), span(3452, 2 * P), span(3708, FG * P)
        gf, ga, yf, ya, mm = slot(0), slot(1), slot(2), slot(3), slot(4)
        xg = slot(5, 2).rearrange("p (a b) -> p a b", a=2)
        hsq = slot(7, 2).rearrange("p (a b) -> p a b", a=2)
        x_in = arena[:, 0:4 * D].rearrange("p (a b) -> p a b", a=4)

        acc = ps("acc", [P, 2, 2, 512])
        score = ps("score", [P, 2, 512])
        turn = ps("turn", [P, 512])
        mixed = ps("mixed", [P, 512])

        const_in, param_in, x_loaded = sem("const_in"), sem("param_in"), sem("x_loaded")
        const_ready = sem("const_ready")
        x_turned = sem("x_turned")
        h_step, h_ready = sem("h_step"), sem("h_ready")
        raw_landed = [sem("raw_landed0"), sem("raw_landed1")]
        w_hi_ready = sem("w_hi_ready")
        w_ready = sem("w_ready")
        tile_done = sem("tile_done")
        tile_taken = sem("tile_taken")
        xg_ready, xh_ready = sem("xg_ready"), sem("xh_ready")
        x_ready = sem("x_ready")
        hsq_ready = sem("hsq_ready")
        hsq_added = sem("hsq_added")
        turn_full, turn_free = sem("turn_full"), sem("turn_free")
        score_full, score_free = sem("score_full"), sem("score_free")
        mixed_full, mixed_free = sem("mixed_full"), sem("mixed_free")
        ms_ready = sem("ms_ready")
        rs_ready = sem("rs_ready")
        diag_ready = sem("diag_ready")
        rot_loaded, rot_ready = sem("rot_loaded"), sem("rot_ready")
        swapped = sem("swapped")
        rsq_ready = sem("rsq_ready")
        rope_a, rope_b = sem("rope_a"), sem("rope_b")
        rope_ready = sem("rope_ready")
        kscaled = sem("kscaled")
        rope_hi = sem("rope_hi")
        rope_done = sem("rope_done")
        v_hi_ready, v_ready = sem("v_hi_ready"), sem("v_ready")
        max_ready, bias_ready = sem("max_ready"), sem("bias_ready")
        rinv_ready, prob_ready = sem("rinv_ready"), sem("prob_ready")
        pt_hi_ready = sem("pt_hi_ready")
        tail_hi_ready = sem("tail_hi_ready")
        tanh_ready = sem("tanh_ready")
        silu_ready = sem("silu_ready")
        att_ready, att_hi_ready = sem("att_ready"), sem("att_hi_ready")
        att_done = sem("att_done")
        ft_loaded, ft_hi_ready, ft_ready = sem("ft_loaded"), sem("ft_hi_ready"), sem("ft_ready")
        fold_zero, folded, fold_hi_ready = sem("fold_zero"), sem("folded"), sem("fold_hi_ready")
        fold_ready = sem("fold_ready")
        pq_hi_ready, pq_ready = sem("pq_hi_ready"), sem("pq_ready")
        fb_ready, fgate_ready, z_gated, z_hi_ready = (sem("fb_ready"), sem("fgate_ready"), sem("z_gated"),
                                                      sem("z_hi_ready"))
        z_ready = sem("z_ready")
        m_hi_ready = sem("m_hi_ready")
        m_done = sem("m_done")
        m_ready = sem("m_ready")
        out_turned, out_ready, out_stored = sem("out_turned"), sem("out_ready"), sem("out_stored")

        waited = sem("waited")

        block = ctx.enter_context(nc.Block())

        def halves(flat):
            return flat.rearrange("p (a b) -> p a b", a=2)

        def flat(t):
            return t.rearrange("p a b -> p (a b)")

        def wait_apart(eng, semaphore, value):
            eng.wait_ge(semaphore, value)
            eng.sem_inc(waited, 1)

        def slot_of(T, odd):
            return T % 2 if odd is None else odd

        @block.sync
        def _(sp):
            sp.dma_start(ident[:], eye).then_inc(const_in, 16)
            for t in range(4):
                sp.dma_start(x_in[:, t, :], x[0, t * P:(t + 1) * P, :]).then_inc(x_loaded, 16)
            sp.dma_start(arena[0:META, 4 * D:5 * D], meta).then_inc(x_loaded, 16)

            def load(l, T, w, col, odd=None, rows=D):
                s = slot_of(T, odd)
                wait_apart(sp, w_ready, l * TL + T + 1)
                sp.dma_start(w_raw[:, s, 0:rows // P, :],
                             w[l, :, bass.ds(col, P)].rearrange("(k p) f -> p k f", p=P)
                             ).then_inc(raw_landed[s], 16)

            def swap(l, T, unit):
                wait_apart(sp, tile_taken, l * TL + T + 3)
                wait_apart(sp, rope_ready, l * ROPES + unit + 1)
                for q in range(4):
                    a, b = q * QUARTER, (q ^ 1) * QUARTER
                    sp.dma_start(rp_swap[a:a + QUARTER, :], rp_raw[b:b + QUARTER, :]).then_inc(swapped, 16)

            with sp.Fori(0, DEPTH) as l:
                load(l, T_K0, w_in, C_K)
                load(l, T_Q0, w_in, C_Q)
                wait_apart(sp, rope_done, l * ROPES + 1)
                sp.dma_start(rot[:, 0:2, :], rope).then_inc(rot_loaded, 16)
                sp.dma_start(rot[:, 2:4, :], rope).then_inc(rot_loaded, 16)
                load(l, T_K1, w_in, C_K + P)
                load(l, T_V0, w_in, C_V)
                swap(l, T_K0, 0)
                load(l, T_V1, w_in, C_V + P)
                swap(l, T_Q0, 1)
                load(l, T_HEAD, w_in, C_Q + P)
                swap(l, T_K1, 2)
                load(l, T_HEAD + 1, w_in, C_AGATE)
                with sp.Fori(1, HEADS - 1) as h:
                    load(l, T_HEAD + 2 * h, w_in, C_Q + P + P * h, odd=1)
                    load(l, T_HEAD + 1 + 2 * h, w_in, C_AGATE + P * h, odd=0)
                    swap(l, T_HEAD - 2 + 2 * h, 2 + h)
                load(l, T_AG7, w_in, C_AGATE + 7 * P)
                load(l, T_FG0, w_in, C_FGATE)
                swap(l, T_HEAD - 2 + 2 * 7, 9)
                load(l, T_FOUR, w_in, C_FVAL)
                wait_apart(sp, rope_done, l * ROPES + ROPES + 1)
                wait_apart(sp, silu_ready, l * HEADS + HEADS)
                wait_apart(sp, turn_full, l * UL + U_QM + 1)
                sp.dma_start(ft_raw[0:FT, :], dft_pos).then_inc(ft_loaded, 16)
                sp.dma_start(ch_raw, dft_ch).then_inc(ft_loaded, 16)
                sp.dma_start(fm_raw.rearrange("p (g c) -> p g c", g=FG),
                             w_fmix[l].rearrange("g d c -> d g c")).then_inc(ft_loaded, 16)
                load(l, T_FOUR + 1, w_in, C_FGATE + P)
                with sp.Fori(1, FG - 1) as g:
                    load(l, T_FOUR + 2 * g, w_in, C_FVAL + P * g, odd=1)
                    load(l, T_FOUR + 1 + 2 * g, w_in, C_FGATE + P + P * g, odd=0)
                load(l, T_FV3, w_in, C_FVAL + 3 * P)
                with sp.Fori(0, NC) as j:
                    load(l, T_MIX + 4 * j, w_in, C_GF + P * j, odd=0)
                    load(l, T_MIX + 1 + 4 * j, w_in, C_GA + P * j, odd=1)
                    load(l, T_MIX + 2 + 4 * j, w_fproj, P * j, odd=0, rows=FG * P)
                    load(l, T_MIX + 3 + 4 * j, w_aproj, P * j, odd=1)
                with sp.Fori(0, NC // 2) as j:
                    load(l, T_OUT + 2 * j, w_out, 2 * P * j, odd=0)
                    load(l, T_OUT + 1 + 2 * j, w_out, P + 2 * P * j, odd=1)
            for t in range(ROW_TILES):
                sp.wait_ge(out_ready, 2 * (t + 1))
                sp.dma_start(out[0, t * P:(t + 1) * P, :], x_in[:, t, :]).then_inc(out_stored, 16)
            sp.wait_ge(out_stored, 16 * ROW_TILES)

        @block.tensor
        def _(pe):
            def passes(dst, whi, wlo, mhi, mlo, first, last, done=None):
                for n, (w, m) in enumerate(((wlo, mhi), (whi, mlo), (whi, mhi))):
                    for b in range(len(dst)):
                        i = pe.matmul(dst[b], w, m[b], start=first and n == 0, stop=last and n == 2)
                if done is not None:
                    i.then_inc(done, 1)

            def cols(t):
                return [t[:, 0:HALF], t[:, HALF:S]]

            def tile(l, T, k0=0, k1=NC, odd=None, hi=x_hi, lo=x_lo, chunks=NC, ahead=None):
                s = slot_of(T, odd)
                if k0 == 0:
                    pe.wait_ge(w_ready, l * TL + T + 3)
                    pe.wait_ge(tile_taken, l * TL + T + 1)
                for k in range(k0, min(k1, chunks)):
                    if ahead is not None:
                        ahead(k)
                    passes([acc[:, s, 0, 0:HALF], acc[:, s, 1, 0:HALF]], w_hi[:, s, k, :], w_lo[:, s, k, :],
                           cols(hi[:, k, :]), cols(lo[:, k, :]), k == 0, k == chunks - 1,
                           tile_done if k == chunks - 1 else None)

            def sum_squares(l, use, src):
                pe.wait_ge(turn_free, l * UL + use + 1)
                for t in range(NP_):
                    i = pe.matmul(turn[0:NT, t:t + 1], src[:, NT * t:NT * (t + 1)], ones[:, 0:1],
                                  start=True, stop=True)
                i.then_inc(turn_full, 1)

            def broadcast(l, n, use):
                pe.wait_ge(diag_ready, l * NORMS + n + 1)
                pe.wait_ge(score_free, l * WL + use + 1)
                for t in range(NP_):
                    c = NT * (t % 3)
                    i = pe.matmul(score[:, t // 3, c:c + NT], ones[0:NT, :],
                                  diag[0:NT, NT * t:NT * (t + 1)], start=True, stop=True)
                i.then_inc(score_full, 1)

            def turn_values(l, kv):
                pe.wait_ge(tile_taken, l * TL + T_V0 + kv + 3)
                pe.wait_ge(turn_free, l * UL + U_V0 + kv + 1)
                pe.wait_ge(mixed_free, l * OL + O_V0 + kv + 1)
                for c in range(4):
                    i = pe.transpose(turn[:, c * P:(c + 1) * P], v_t[:, kv, c * P:(c + 1) * P], ident[:])
                i.then_inc(turn_full, 1)
                pe.transpose(mixed[0:META, 0:P], v_t[:, kv, TAIL:S], ident[:]).then_inc(mixed_full, 1)

            def q_norm(l, use, unit):
                pe.wait_ge(rsq_ready, l * ROPES + unit + 2)
                pe.wait_ge(turn_free, l * UL + use + 1)
                for t in range(ROW_TILES):
                    i = pe.matmul(turn[:, t:t + 1], rp_sq[:, META + P * t:META + P * (t + 1)], ones[:, 0:1],
                                  start=True, stop=True)
                i.then_inc(turn_full, 1)

            def scores(l, use, qhi, qlo, kv, n):
                pe.wait_ge(score_free, l * WL + use + 1)
                passes([score[0:n, 0, 0:HALF], score[0:n, 1, 0:HALF]], qhi, qlo,
                       cols(k_hi[:, kv, :]), cols(k_lo[:, kv, :]), True, True, score_full)

            def turn_probs(l, q, use, s, n, tail_at, tail_last):
                pe.wait_ge(turn_free, l * UL + use + 1)
                wait_apart(pe, prob_ready, l * QTL + q + 1)
                i = pe.transpose(mixed[0:META, tail_at:tail_at + n], prob[0:n, s, TAIL:S], ident[0:n, 0:n])
                if tail_last:
                    i.then_inc(mixed_full, 1)
                for c in range(4):
                    i = pe.transpose(turn[:, c * n:(c + 1) * n], prob[0:n, s, c * P:(c + 1) * P], ident[0:n, 0:n])
                i.then_inc(turn_full, 1)

            def weigh_values(l, use, last_use, kv, n):
                pe.wait_ge(turn_free, l * UL + last_use + 2)
                pe.wait_ge(mixed_free, l * OL + use + 1)
                for c in range(KCH):
                    rows = P if c < 4 else META
                    hi = pt_hi[:, c, 0:n] if c < 4 else tail_hi[0:META, 0:n]
                    lo = pt_lo[:, c, 0:n] if c < 4 else tail_lo[0:META, 0:n]
                    passes([mixed[:, 0:n]], v_hi[0:rows, kv, c, :], v_lo[0:rows, kv, c, :], [hi], [lo],
                           c == 0, c == KCH - 1, mixed_full if c == KCH - 1 else None)

            def query(l, w, t, kv):
                a = META + P * t
                scores(l, w + t, q_hi[:, a:a + P], q_lo[:, a:a + P], kv, P)

            def turned(l, q, u, o, t):
                if t == 0:
                    pe.wait_ge(mixed_free, l * OL + o + 1)
                turn_probs(l, q + t, u + t, t % 2, P, P * t, t == 3)

            def head(l, h, kv):
                A, B = T_HEAD + 2 * h, T_HEAD + 1 + 2 * h
                u, w, o, q = U_HEAD + 5 * h, W_HEAD + 4 * h, O_HEAD + 2 * h, 4 * h
                pe.wait_ge(rope_done, l * ROPES + h + 4)
                query(l, w, 0, kv)
                tile(l, A, 0, 4, odd=1)
                query(l, w, 1, kv)
                turned(l, q, u, o, 0)
                tile(l, A, 4, NC, odd=1)
                query(l, w, 2, kv)
                turned(l, q, u, o, 1)
                tile(l, B, 0, 4, odd=0)
                query(l, w, 3, kv)
                turned(l, q, u, o, 2)
                tile(l, B, 4, 6, odd=0)
                turned(l, q, u, o, 3)
                tile(l, B, 6, NC, odd=0)
                q_norm(l, u + 4, 3 + h)
                weigh_values(l, o + 1, u + 3, kv, 4 * P)

            def last_head(l):
                A, B = T_AG7, T_FG0
                pe.wait_ge(rope_done, l * ROPES + ROPES + 1)
                pe.wait_ge(turn_free, l * UL + U_QM + 1)
                for kv in range(KV):
                    i = pe.matmul(turn[0:4 * META, kv:kv + 1], flat(qm_sq[:, 4 * kv:4 * kv + 4, :]),
                                  ones[:, 0:1], start=True, stop=True)
                i.then_inc(turn_full, 1)
                for kv in range(KV):
                    o = O_M0 + 2 * kv
                    scores(l, W_M0 + kv, flat(qm_hi[:, 4 * kv:4 * kv + 4, :]), flat(qm_lo[:, 4 * kv:4 * kv + 4, :]),
                           kv, 4 * META)
                    tile(l, A, 4 * kv, 4 * kv + 2, odd=1)
                    pe.wait_ge(mixed_free, l * OL + o + 1)
                    turn_probs(l, QT_M0 + kv, U_M0 + kv, kv, 4 * META, 0, True)
                    tile(l, A, 4 * kv + 2, 4 * kv + 4, odd=1)
                    weigh_values(l, o + 1, U_M0 + kv, kv, 4 * META)
                u, w, o, q = U_H7, W_H7, O_H7, QT_H7
                query(l, w, 0, 1)
                tile(l, B, 0, 2, odd=0)
                query(l, w, 1, 1)
                turned(l, q, u, o, 0)
                tile(l, B, 2, 4, odd=0)
                query(l, w, 2, 1)
                turned(l, q, u, o, 1)
                tile(l, B, 4, 5, odd=0)
                query(l, w, 3, 1)
                turned(l, q, u, o, 2)
                tile(l, B, 5, 6, odd=0)
                turned(l, q, u, o, 3)
                tile(l, B, 6, NC, odd=0)
                weigh_values(l, o + 1, u + 3, 1, 4 * P)

            def channels(l, g):
                pe.wait_ge(fold_ready, l * FG + g + 2)
                pe.wait_ge(score_free, l * WL + W_F + g + 1)
                for part in range(2):
                    for c in range(FCH):
                        a = slice(FT * c, FT * (c + 1))
                        passes([score[0:FT, part, P * c:P * (c + 1)]], xf_hi[:, part, a], xf_lo[:, part, a],
                               [cw_hi[:, part, g, :]], [cw_lo[:, part, g, :]], True, True,
                               score_full if part and c == FCH - 1 else None)

            def positions(l, g):
                pe.wait_ge(pq_ready, l * FG + g + 1)
                for part, (bank, free, full, use) in enumerate(((turn, turn_free, turn_full, l * UL + U_A),
                                                               (mixed, mixed_free, mixed_full, l * OL + O_B))):
                    pe.wait_ge(free, use + g + 1)
                    for c in range(FCH):
                        r = part * FCH + c
                        passes([bank[:, 0:FS]], pq_hi[0:FT, r, :], pq_lo[0:FT, r, :],
                               [ft_hi[0:FT, part, c, :]], [ft_lo[0:FT, part, c, :]], c == 0, c == FCH - 1,
                               full if c == FCH - 1 else None)

            pe.sem_inc(tile_done, 2)
            pe.wait_ge(const_in, 16)
            pe.wait_ge(x_loaded, 80)
            for c in range(NC):
                if c >= 2:
                    pe.wait_ge(h_ready, c - 1)
                for t in range(4):
                    pe.transpose(acc[:, c % 2, 0, t * P:(t + 1) * P], x_in[:, t, c * P:(c + 1) * P], ident[:])
                pe.transpose(acc[:, c % 2, 1, 0:META], arena[0:META, 4 * D + c * P:4 * D + (c + 1) * P],
                             ident[0:META, 0:META]).then_inc(x_turned, 1)
            pe.wait_ge(h_ready, NC)
            pe.wait_ge(const_ready, 4)

            with pe.Fori(0, DEPTH) as l:
                def x_chunk(k):
                    pe.wait_ge(x_ready, l * NC + k + 3)
                tile(l, T_K0, 0, 6, ahead=x_chunk)
                pe.wait_ge(hsq_added, l * NC + NC + 2)
                sum_squares(l, U_RMS, sqsum)
                tile(l, T_K0, 6, NC, ahead=x_chunk)
                tile(l, T_Q0, 0, 4)
                broadcast(l, 0, W_RMS)
                tile(l, T_Q0, 4, NC)
                tile(l, T_K1, 0, 4)
                pe.wait_ge(rsq_ready, l * ROPES + 2)
                sum_squares(l, U_K0, rp_sq)
                tile(l, T_K1, 4, NC)
                tile(l, T_V0, 0, 4)
                broadcast(l, 1, W_K0)
                q_norm(l, U_Q0, 1)
                tile(l, T_V0, 4, NC)
                tile(l, T_V1, 0, 6)
                pe.wait_ge(rsq_ready, l * ROPES + 4)
                sum_squares(l, U_K1, rp_sq)
                tile(l, T_V1, 6, NC)
                broadcast(l, 2, W_K1)
                turn_values(l, 0)
                turn_values(l, 1)
                wait_apart(pe, v_ready, l * KV + KV)
                with pe.Fori(0, GQA) as h:
                    head(l, h, 0)
                with pe.Fori(GQA, HEADS - 1) as h:
                    head(l, h, 1)
                last_head(l)

                pe.wait_ge(ft_loaded, l * 48 + 48)
                pe.wait_ge(turn_free, l * UL + U_CW + 1)
                pe.matmul(turn[:, :], ch_raw[:, 0:P], fm_raw, start=True, stop=True).then_inc(turn_full, 1)
                pe.wait_ge(mixed_free, l * OL + O_SW + 1)
                pe.matmul(mixed[:, :], ch_raw[:, P:2 * P], fm_raw, start=True, stop=True).then_inc(mixed_full, 1)
                with pe.Fori(0, FG - 1) as g:
                    tile(l, T_FOUR + 2 * g, odd=1)
                    tile(l, T_FOUR + 1 + 2 * g, 0, 6, odd=0)
                    pe.wait_ge(ft_ready, l * 3 + 3)
                    channels(l, g)
                    tile(l, T_FOUR + 1 + 2 * g, 6, NC, odd=0)
                    positions(l, g)
                tile(l, T_FV3)
                channels(l, FG - 1)
                positions(l, FG - 1)

                wait_apart(pe, att_done, l * ATT + ATT + 1)
                with pe.Fori(0, NC) as j:
                    tile(l, T_MIX + 4 * j, odd=0)
                    tile(l, T_MIX + 1 + 4 * j, odd=1)
                    pe.wait_ge(z_ready, l * FG + FG + 1)
                    tile(l, T_MIX + 2 + 4 * j, odd=0, hi=z_hi, lo=z_lo, chunks=FG)
                    tile(l, T_MIX + 3 + 4 * j, odd=1, hi=att_hi, lo=att_lo)
                with pe.Fori(0, NC // 2) as j:
                    tile(l, T_OUT + 2 * j, odd=0, hi=m_hi, lo=m_lo,
                         ahead=lambda k: pe.wait_ge(m_done, l * NC + k + 2))
                    tile(l, T_OUT + 1 + 2 * j, odd=1, hi=m_hi, lo=m_lo)

            pe.wait_ge(tile_taken, DEPTH * TL + 2)
            for n in range(2 * ROW_TILES):
                t, half = n // 2, n % 2
                if n >= 2:
                    pe.wait_ge(out_ready, n - 1)
                for c in range(4):
                    i = pe.transpose(acc[:, n % 2, 0, c * P:(c + 1) * P],
                                     h_t[:, 4 * half + c, META + t * P:META + (t + 1) * P], ident[:])
                i.then_inc(out_turned, 1)

        @block.scalar
        def _(act):
            def split_hi(l, T, odd=None, n=NC):
                s = slot_of(T, odd)
                act.wait_ge(raw_landed[s], 8 * TL * l + 8 * (T - s) + 16)
                act.wait_ge(tile_done, l * TL + T + 1)
                act.activation(w_hi[:, s, 0:n, :], w_raw[:, s, 0:n, :], ACT.Copy).then_inc(w_hi_ready, 1)

            def absorb(n, c, s):
                act.wait_ge(xg_ready, n + 1)
                act.activation(x_hi[:, c, :], xg[:, s, :], ACT.Copy).then_inc(xh_ready, 1)
                act.wait_ge(hsq_added, n + 1)
                act.activation(hsq[:, s, :], h_t[:, c, :], ACT.Square).then_inc(hsq_ready, 1)

            def square(l, T, norm_use):
                act.wait_ge(tile_taken, l * TL + T + 3)
                act.wait_ge(turn_full, l * UL + norm_use + 1)
                act.activation(rp_sq, rp_raw, ACT.Square).then_inc(rsq_ready, 1)

            def q_square(l, T, norm_use, h):
                act.wait_ge(tile_taken, l * TL + T + 3)
                act.activation(qm_sq[:, h, :], rp_raw[:, 0:META], ACT.Square)
                square(l, T, norm_use)

            def k_hi_part(l, kv, n):
                act.wait_ge(kscaled, l * KV + kv + 1)
                act.activation(k_hi[:, kv, :], rp_b, ACT.Copy).then_inc(rope_hi, 1)

            def q_hi_part(l, h, unit):
                act.wait_ge(rope_ready, l * ROPES + unit + 2)
                act.activation(qm_hi[:, h, :], rp_a[:, 0:META], ACT.Copy)
                act.activation(q_hi, rp_a, ACT.Copy).then_inc(rope_hi, 1)

            def value_hi(l, kv):
                act.wait_ge(turn_full, l * UL + U_V0 + kv + 1)
                act.wait_ge(mixed_full, l * OL + O_V0 + kv + 1)
                act.activation(v_hi[0:META, kv, 4, :], mixed[0:META, 0:P], ACT.Copy)
                act.activation(v_hi[:, kv, 0:4, :], turn[:, :].rearrange("p (c d) -> p c d", c=4),
                               ACT.Copy).then_inc(v_hi_ready, 1)

            def exps(l, q, s, n, col, slot_use):
                act.wait_ge(bias_ready, l * QTL + q + 1)
                act.wait_ge(turn_full, l * UL + slot_use + 1)
                act.activation(halves(prob[0:n, s, :]), score[0:n, :, 0:HALF], ACT.Exp, bias=nbias[0:n, s:s + 1],
                               scale=rs[0:n, col:col + 1], accum_out=rsum[0:n, s:s + 1]).then_inc(score_free, 1)

            def probs_hi(l, use, n, at, o):
                act.wait_ge(turn_full, l * UL + use + 1)
                act.wait_ge(mixed_full, l * OL + o)
                act.activation(pt_hi[:, :, at:at + n], turn[:, 0:4 * n].rearrange("p (c q) -> p c q", c=4),
                               ACT.Copy).then_inc(pt_hi_ready, 1)

            def tail_hi_part(l, o, n):
                act.wait_ge(mixed_full, l * OL + o + 1)
                act.activation(tail_hi[0:META, 0:n], mixed[0:META, 0:n], ACT.Copy).then_inc(tail_hi_ready, 1)

            def gate_tanh(l, T, src):
                act.wait_ge(tile_taken, l * TL + T + 3)
                act.activation(ag_th, src, ACT.Tanh, scale=0.5).then_inc(tanh_ready, 1)

            def att_hi_part(l, n, dst, src):
                act.wait_ge(att_ready, l * ATT + n + 1)
                act.activation(dst, src, ACT.Copy).then_inc(att_hi_ready, 1)

            def head(l, h):
                u, o, q = U_HEAD + 5 * h, O_HEAD + 2 * h, 4 * h
                exps(l, q, 0, P, Q_COL, u - 3)
                exps(l, q + 1, 1, P, Q_COL + 1, u - 2)
                probs_hi(l, u, P, 0, o)
                split_hi(l, T_HEAD + 2 + 2 * h, odd=1)
                q_square(l, T_HEAD + 2 * h, u - 1, h + 1)
                exps(l, q + 2, 0, P, Q_COL + 2, u)
                probs_hi(l, u + 1, P, P, o)
                exps(l, q + 3, 1, P, Q_COL + 3, u + 1)
                probs_hi(l, u + 2, P, 2 * P, o)
                probs_hi(l, u + 3, P, 3 * P, o)
                tail_hi_part(l, o, 4 * P)
                q_hi_part(l, h + 1, 3 + h)
                split_hi(l, T_HEAD + 3 + 2 * h, odd=0)
                gate_tanh(l, T_HEAD + 1 + 2 * h, ag_raw)
                att_hi_part(l, h, att_hi[:, h, META:S], att[:, META:S])

            def last_head(l):
                for kv in range(KV):
                    exps(l, QT_M0 + kv, kv, 4 * META, M_COL + kv, U_HEAD + 5 * 6 + 2 + kv)
                    probs_hi(l, U_M0 + kv, 4 * META, 0, O_M0 + 2 * kv)
                    tail_hi_part(l, O_M0 + 2 * kv, 4 * META)
                    if kv == 0:
                        att_hi_part(l, A_M0, att_hi[:, 0:4, 0:META],
                                    att[:, 0:4 * META].rearrange("p (a b) -> p a b", a=4))
                split_hi(l, T_FOUR)
                gate_tanh(l, T_AG7, ag_raw)
                att_hi_part(l, A_M0 + 1, att_hi[:, 4:8, 0:META], att[:, 0:4 * META].rearrange("p (a b) -> p a b", a=4))
                u, o, q = U_H7, O_H7, QT_H7
                exps(l, q, 0, P, Q_COL, U_M0)
                exps(l, q + 1, 1, P, Q_COL + 1, U_M1)
                probs_hi(l, u, P, 0, o)
                exps(l, q + 2, 0, P, Q_COL + 2, u)
                probs_hi(l, u + 1, P, P, o)
                exps(l, q + 3, 1, P, Q_COL + 3, u + 1)
                probs_hi(l, u + 2, P, 2 * P, o)
                probs_hi(l, u + 3, P, 3 * P, o)
                tail_hi_part(l, o, 4 * P)
                split_hi(l, T_FOUR + 1)
                gate_tanh(l, T_FG0, fgate[:, 0, :])
                att_hi_part(l, A_H7, att_hi[:, 7, META:S], att[:, META:S])

            def fourier(l, g, gate):
                act.wait_ge(folded, l * FG + g + 1)
                act.wait_ge(score_full, l * WL + W_F + g)
                act.activation(xf_hi, fold, ACT.Copy).then_inc(fold_hi_ready, 1)
                act.wait_ge(score_full, l * WL + W_F + g + 1)
                act.wait_ge(mixed_full, l * OL + O_B + g)
                act.activation(pq_hi[0:FT, :, :].rearrange("p (a c) n -> p a (c n)", a=2), score[0:FT, :, 0:FCH * P],
                               ACT.Copy).then_inc(pq_hi_ready, 1)
                if gate:
                    split_hi(l, T_FOUR + 3 + 2 * g, odd=0)
                    gate_tanh(l, T_FOUR + 1 + 2 * g, fgate[:, g + 1, :])
                act.wait_ge(mixed_full, l * OL + O_B + g + 1)
                act.wait_ge(z_hi_ready, l * FG + g + 1)
                act.activation(fb[:, 0:FOLD + 1], mixed[:, 0:FOLD + 1], ACT.Copy).then_inc(mixed_free, 1)
                act.wait_ge(z_gated, l * FG + g + 1)
                act.activation(z_hi[:, g, :], fz, ACT.Copy).then_inc(z_hi_ready, 1)

            act.sem_inc(z_hi_ready, 1)
            for c in range(NC):
                absorb(c, c, c % 2)
            with act.Fori(0, DEPTH) as l:
                split_hi(l, T_K0)
                split_hi(l, T_Q0)
                split_hi(l, T_K1)
                square(l, T_K0, U_RMS)
                split_hi(l, T_V0)
                q_square(l, T_Q0, U_K0, 0)
                k_hi_part(l, 0, 0)
                split_hi(l, T_V1)
                q_hi_part(l, 0, 1)
                square(l, T_K1, U_Q0)
                split_hi(l, T_HEAD)
                k_hi_part(l, 1, 2)
                split_hi(l, T_HEAD + 1)
                value_hi(l, 0)
                value_hi(l, 1)
                with act.Fori(0, HEADS - 1) as h:
                    head(l, h)
                last_head(l)
                act.wait_ge(ft_loaded, l * 48 + 48)
                act.wait_ge(mixed_full, l * OL + O_SW)
                act.activation(ft_hi[0:FT], ft_raw[0:FT, :].rearrange("p (a b c) -> p a b c", a=2, b=FCH),
                               ACT.Copy).then_inc(ft_hi_ready, 1)
                act.wait_ge(turn_full, l * UL + U_CW + 1)
                act.activation(cw_hi[:, 0], turn[:, :].rearrange("p (g c) -> p g c", g=FG),
                               ACT.Copy).then_inc(ft_hi_ready, 1)
                act.wait_ge(mixed_full, l * OL + O_SW + 1)
                act.activation(cw_hi[:, 1], mixed[:, :].rearrange("p (g c) -> p g c", g=FG),
                               ACT.Copy).then_inc(ft_hi_ready, 1)
                with act.Fori(0, FG - 1) as g:
                    split_hi(l, T_FOUR + 2 + 2 * g, odd=1)
                    fourier(l, g, True)
                split_hi(l, T_MIX + 1)
                fourier(l, FG - 1, False)
                with act.Fori(0, NC) as j:
                    T = T_MIX + 4 * j
                    for b, g in ((0, gf), (1, ga)):
                        if b == 0:
                            split_hi(l, T + 2, odd=0, n=FG)
                        else:
                            split_hi(l, T + 3, odd=1)
                        act.wait_ge(tile_taken, l * TL + T + b + 3)
                        act.activation(g, g, ACT.Tanh, scale=0.5,
                                       bias=bhalf[:, l, bass.ds(NC * b + j, 1)]).then_inc(tanh_ready, 1)
                    split_hi(l, T + 4, odd=0)
                    split_hi(l, T + 5, odd=1)
                    act.wait_ge(m_ready, l * NC + j + 2)
                    act.activation(m_hi[:, j, :], mm, ACT.Copy).then_inc(m_hi_ready, 1)
                with act.Fori(0, NC // 2 - 1) as j:
                    for b in range(2):
                        split_hi(l, T_OUT + 2 + 2 * j + b, odd=b)
                        absorb(l * NC + NC + 2 * j + b, 2 * j + b, b)
                for b in range(2):
                    absorb(l * NC + 2 * NC - 2 + b, NC - 2 + b, b)

        @block.vector
        def _(dve):
            def split_lo(l, T, odd=None, n=NC):
                s = slot_of(T, odd)
                dve.wait_ge(w_hi_ready, l * TL + T + 1)
                dve.tensor_tensor(w_lo[:, s, 0:n, :], w_raw[:, s, 0:n, :], w_hi[:, s, 0:n, :].bitcast(F32),
                                  ALU.subtract).then_inc(w_ready, 1)

            def result(s):
                return acc[:, s, :, 0:HALF]

            def take(l, T, dst, odd=None):
                dve.wait_ge(tile_done, l * TL + T + 3)
                dve.tensor_tensor(halves(dst), result(slot_of(T, odd)), halves(rstd[:]), ALU.mult).then_inc(tile_taken, 1)

            def take_rope(l, T, unit, odd=None):
                dve.wait_ge(rsq_ready, l * ROPES + unit + 1)
                dve.wait_ge(rope_ready, l * ROPES + unit + 1)
                take(l, T, rp_raw, odd)

            def absorb(n, gain_l, c, s):
                dve.wait_ge(x_ready, n + 1)
                dve.tensor_scalar(xg[:, s, :], h_t[:, c, :], ngain[:, gain_l, bass.ds(c, 1)], None,
                                  ALU.mult).then_inc(xg_ready, 1)

            def mean_squares(l, use, r, rows, at, n, scale, eps):
                dve.wait_ge(turn_full, l * UL + use + 1)
                dve.wait_ge(rs_ready, l * RL + r + 1)
                dve.tensor_scalar(ms[0:rows, at:at + n], turn[0:rows, 0:n], scale, eps, ALU.mult, ALU.add
                                  ).then_inc(turn_free, 1)
                dve.wait_ge(turn_free, l * UL + use + 2)
                dve.nop().then_inc(ms_ready, 1)

            def diagonals(l, r, n):
                dve.wait_ge(rs_ready, l * RL + r + 2)
                for t in range(NP_):
                    i = dve.tensor_scalar(diag[0:NT, NT * t:NT * (t + 1)], ident[0:NT, 0:NT], rs[0:NT, t:t + 1],
                                          None, ALU.mult)
                i.then_inc(diag_ready, 1)

            def rotate(l, unit, table):
                dve.wait_ge(rope_done, l * ROPES + unit + 1)
                dve.wait_ge(tile_taken, l * TL + unit + 3 if isinstance(unit, int) else l * TL + 2 * unit + 1)
                dve.tensor_tensor(rp_a, rp_raw, rot[:, table, :], ALU.mult).then_inc(rope_a, 1)

            def scale_k(l, kv, unit, n, use):
                dve.wait_ge(rope_ready, l * ROPES + unit + 2)
                dve.wait_ge(score_full, l * WL + use + 1)
                dve.tensor_tensor(halves(rp_b), score[:, :, 0:HALF], halves(rp_a), ALU.mult).then_inc(score_free, 1)
                dve.wait_ge(score_free, l * WL + use + 2)
                dve.nop().then_inc(kscaled, 1)

            def value_lo(l, kv):
                dve.wait_ge(v_hi_ready, l * KV + kv + 1)
                dve.tensor_tensor(v_lo[0:META, kv, 4, :], mixed[0:META, 0:P], v_hi[0:META, kv, 4, :].bitcast(F32),
                                  ALU.subtract).then_inc(mixed_free, 1)
                dve.tensor_tensor(v_lo[:, kv, 0:4, :], turn[:, :].rearrange("p (c d) -> p c d", c=4),
                                  v_hi[:, kv, 0:4, :].bitcast(F32), ALU.subtract).then_inc(turn_free, 1)
                dve.wait_ge(turn_free, l * UL + U_V0 + kv + 2)
                dve.nop().then_inc(v_ready, 1)

            def maximum(l, w, q, s, n, col, r):
                dve.wait_ge(score_full, l * WL + w + 1)
                dve.tensor_reduce(rmax[0:n, s:s + 1], score[0:n, :, 0:HALF], AX.XY, ALU.max).then_inc(max_ready, 1)
                dve.wait_ge(max_ready, l * QTL + q + 1)
                dve.wait_ge(rs_ready, l * RL + r + 2)
                dve.tensor_scalar(nbias[0:n, s:s + 1], rmax[0:n, s:s + 1], rs[0:n, col:col + 1], -1.0,
                                  ALU.mult, ALU.mult).then_inc(bias_ready, 1)

            def inverse(l, w, s, n):
                dve.wait_ge(score_free, l * WL + w + 2)
                dve.reciprocal(rinv[0:n, s:s + 1], rsum[0:n, s:s + 1]).then_inc(rinv_ready, 1)

            def probs_lo(l, q, n, at):
                dve.wait_ge(pt_hi_ready, l * QTL + q + 1)
                dve.tensor_tensor(pt_lo[:, :, at:at + n], turn[:, 0:4 * n].rearrange("p (c q) -> p c q", c=4),
                                  pt_hi[:, :, at:at + n].bitcast(F32), ALU.subtract).then_inc(turn_free, 1)

            def tail_lo_part(l, n_tail, n):
                dve.wait_ge(tail_hi_ready, l * ATT + n_tail + 1)
                dve.tensor_tensor(tail_lo[0:META, 0:n], mixed[0:META, 0:n], tail_hi[0:META, 0:n].bitcast(F32),
                                  ALU.subtract).then_inc(mixed_free, 1)

            def silus(l, T, h):
                dve.wait_ge(tanh_ready, l * HL + h + 1)
                dve.wait_ge(tile_taken, l * TL + T + 3)
                dve.scalar_tensor_tensor(agm[:, h, :], ag_th[:, 0:META], 1.0, ag_raw[:, 0:META], ALU.add, ALU.mult)
                dve.scalar_tensor_tensor(silu, ag_th, 1.0, ag_raw, ALU.add, ALU.mult).then_inc(silu_ready, 1)

            def output(l, n, o, dst, src, gate):
                dve.wait_ge(mixed_full, l * OL + o + 1)
                dve.wait_ge(att_done, l * ATT + n + 1)
                dve.scalar_tensor_tensor(dst, src, 0.5, gate, ALU.mult, ALU.mult).then_inc(mixed_free, 1)
                dve.wait_ge(mixed_free, l * OL + o + 2)
                dve.nop().then_inc(att_ready, 1)

            def head(l, h):
                w, o, q = W_HEAD + 4 * h, O_HEAD + 2 * h, 4 * h
                r = R_Q0 if isinstance(h, int) and h == 0 else R_QNEXT - 1 + h
                maximum(l, w, q, 0, P, Q_COL, r)
                inverse(l, w, 0, P)
                maximum(l, w + 1, q + 1, 1, P, Q_COL + 1, r)
                probs_lo(l, q, P, 0)
                inverse(l, w + 1, 1, P)
                take_rope(l, T_HEAD + 2 * h, 3 + h, odd=1)
                split_lo(l, T_HEAD + 2 + 2 * h, odd=1)
                maximum(l, w + 2, q + 2, 0, P, Q_COL + 2, r)
                probs_lo(l, q + 1, P, P)
                inverse(l, w + 2, 0, P)
                rotate(l, 3 + h, 0)
                maximum(l, w + 3, q + 3, 1, P, Q_COL + 3, r)
                probs_lo(l, q + 2, P, 2 * P)
                inverse(l, w + 3, 1, P)
                probs_lo(l, q + 3, P, 3 * P)
                tail_lo_part(l, h, 4 * P)
                take(l, T_HEAD + 1 + 2 * h, ag_raw, odd=0)
                split_lo(l, T_HEAD + 3 + 2 * h, odd=0)
                mean_squares(l, U_HEAD + 5 * h + 4, R_QNEXT + h, P, Q_COL, ROW_TILES, 1.0, HD * EPS)
                silus(l, T_HEAD + 1 + 2 * h, h)
                dve.wait_ge(silu_ready, l * HEADS + h + 1)
                output(l, h, o + 1, att[:, META:S], mixed[:, :], silu[:, META:S])

            def last_head(l):
                mean_squares(l, U_QM, R_QM, 4 * META, M_COL, KV, 1.0, HD * EPS)
                for kv in range(KV):
                    n = 4 * META
                    maximum(l, W_M0 + kv, QT_M0 + kv, kv, n, M_COL + kv, R_QM)
                    inverse(l, W_M0 + kv, kv, n)
                    probs_lo(l, QT_M0 + kv, n, 0)
                    tail_lo_part(l, A_M0 + kv, n)
                    if kv:
                        take(l, T_AG7, ag_raw)
                        split_lo(l, T_FOUR)
                        silus(l, T_AG7, HEADS - 1)
                        dve.wait_ge(silu_ready, l * HEADS + HEADS)
                    output(l, A_M0 + kv, O_M0 + 2 * kv + 1, att[:, 0:n], mixed[:, 0:n], flat(agm[:, 4 * kv:4 * kv + 4, :]))
                w, o, q, r = W_H7, O_H7, QT_H7, R_QM
                maximum(l, w, q, 0, P, Q_COL, r)
                inverse(l, w, 0, P)
                for t in range(1, 4):
                    maximum(l, w + t, q + t, t % 2, P, Q_COL + t, r)
                    probs_lo(l, q + t - 1, P, P * (t - 1))
                    inverse(l, w + t, t % 2, P)
                probs_lo(l, q + 3, P, 3 * P)
                tail_lo_part(l, A_H7, 4 * P)
                take(l, T_FG0, fgate[:, 0, :])
                split_lo(l, T_FOUR + 1)
                fourier_gate(l, T_FG0, 0)
                output(l, A_H7, o + 1, att[:, META:S], mixed[:, :], silu[:, META:S])

            def fourier_gate(l, T, g):
                dve.wait_ge(tanh_ready, l * HL + H_FG + g + 1)
                dve.wait_ge(tile_taken, l * TL + T + 3)
                dve.scalar_tensor_tensor(fgate[:, g, :], ag_th, 1.0, fgate[:, g, :], ALU.add, ALU.mult
                                         ).then_inc(fgate_ready, 1)

            def table_lo(l, n, dst, src, hi, freed):
                dve.wait_ge(ft_hi_ready, l * 3 + n + 1)
                dve.tensor_tensor(dst, src, hi.bitcast(F32), ALU.subtract).then_inc(freed or ft_ready, 1)
                if freed:
                    dve.drain().then_inc(ft_ready, 1)

            def fourier(l, g, T, odd, gate):
                take(l, T, fv, odd)
                split_lo(l, T + 2, odd=odd)
                dve.wait_ge(tile_taken, l * TL + T + 3)
                dve.wait_ge(fold_ready, l * FG + g + 1)
                dve.wait_ge(fold_zero, l + 1)
                dve.tensor_copy(fold[:, 0, 0:FOLD + 1:FOLD], fv[:, 0:FOLD + 1:FOLD])
                dve.tensor_tensor(fold[:, 0, 1:FOLD], fv[:, 1:FOLD], fv[:, S - 1:FOLD:-1], ALU.add)
                dve.tensor_tensor(fold[:, 1, 1:FOLD], fv[:, 1:FOLD], fv[:, S - 1:FOLD:-1],
                                  ALU.subtract).then_inc(folded, 1)
                dve.wait_ge(pq_hi_ready, l * FG + g + 1)
                dve.tensor_tensor(pq_lo[0:FT].rearrange("p (a c) n -> p a (c n)", a=2), score[0:FT, :, 0:FCH * P],
                                  pq_hi[0:FT].rearrange("p (a c) n -> p a (c n)", a=2).bitcast(F32),
                                  ALU.subtract).then_inc(score_free, 1)
                dve.wait_ge(score_free, l * WL + W_F + g + 2)
                dve.nop().then_inc(pq_ready, 1)
                if gate:
                    take(l, T + 1, fgate[:, g + 1, :], odd=0)
                    split_lo(l, T + 3, odd=0)
                    fourier_gate(l, T + 1, g + 1)
                dve.wait_ge(turn_full, l * UL + U_A + g + 1)
                dve.wait_ge(mixed_free, l * OL + O_B + g + 2)
                dve.wait_ge(z_ready, l * FG + g + 1)
                dve.tensor_tensor(fz[:, 0:FOLD + 1], turn[:, 0:FOLD + 1], fb[:, 0:FOLD + 1], ALU.subtract)
                dve.tensor_tensor(fz[:, S - 1:FOLD:-1], turn[:, 1:FOLD], fb[:, 1:FOLD], ALU.add).then_inc(turn_free, 1)
                dve.wait_ge(turn_free, l * UL + U_A + g + 2)
                dve.wait_ge(fgate_ready, l * FG + g + 1)
                dve.scalar_tensor_tensor(fz, fz, 0.5, fgate[:, g, :], ALU.mult, ALU.mult).then_inc(z_gated, 1)

            for s, n in ((w_ready, 2), (tile_taken, 2), (turn_free, 1), (score_free, 1), (mixed_free, 1)):
                dve.sem_inc(s, n)
            dve.memset(ones[:], 1.0).then_inc(const_ready, 1)
            dve.memset(halfneg[:], -0.5).then_inc(const_ready, 1)
            dve.memset(ngain[:, DEPTH, :], 0.0).then_inc(const_ready, 1)
            dve.wait_ge(param_in, 16 * PARAMS)
            dve.tensor_scalar(bhalf[:], bhalf[:], 0.5, None, ALU.mult).then_inc(const_ready, 1)
            for c in range(NC):
                dve.wait_ge(x_turned, c + 1)
                dve.tensor_copy(h_t[:, c, 0:META], acc[:, c % 2, 1, 0:META]).then_inc(h_step, 1)
                dve.tensor_copy(h_t[:, c, META:S], acc[:, c % 2, 0, :]).then_inc(h_ready, 1)
            dve.wait_ge(x_turned, NC)
            dve.wait_ge(h_ready, NC)
            for c in range(NC):
                absorb(c, 0, c, c % 2)

            with dve.Fori(0, DEPTH) as l:
                split_lo(l, T_K0)
                split_lo(l, T_Q0)
                mean_squares(l, U_RMS, R_H, NT, 0, NP_, 1.0 / D, EPS)
                diagonals(l, R_H, 0)
                dve.wait_ge(rot_loaded, l * 32 + 32)
                for n in range(4):
                    i = dve.tensor_scalar(rot[:, n, :], rot[:, n, :], gains[:, l, n:n + 1], None, ALU.mult)
                i.then_inc(rot_ready, 1)
                dve.wait_ge(score_full, l * WL + W_RMS + 1)
                dve.tensor_copy(halves(rstd[:]), score[:, :, 0:HALF]).then_inc(score_free, 1)
                dve.wait_ge(score_free, l * WL + W_RMS + 2)
                take_rope(l, T_K0, 0)
                split_lo(l, T_K1)
                dve.wait_ge(rot_ready, l + 1)
                rotate(l, 0, 2)
                take_rope(l, T_Q0, 1)
                split_lo(l, T_V0)
                mean_squares(l, U_K0, R_K0, NT, 0, NP_, 1.0 / HD, EPS)
                diagonals(l, R_K0, 1)
                scale_k(l, 0, 0, 1, W_K0)
                rotate(l, 1, 0)
                take_rope(l, T_K1, 2)
                split_lo(l, T_V1)
                mean_squares(l, U_Q0, R_Q0, P, Q_COL, ROW_TILES, 1.0, HD * EPS)
                take(l, T_V0, v_t[:, 0, :])
                split_lo(l, T_HEAD)
                rotate(l, 2, 2)
                mean_squares(l, U_K1, R_K1, NT, 0, NP_, 1.0 / HD, EPS)
                diagonals(l, R_K1, 2)
                scale_k(l, 1, 2, 2, W_K1)
                take(l, T_V1, v_t[:, 1, :])
                split_lo(l, T_HEAD + 1)
                value_lo(l, 0)
                value_lo(l, 1)
                with dve.Fori(0, HEADS - 1) as h:
                    head(l, h)
                last_head(l)
                dve.wait_ge(att_ready, l * ATT + ATT)
                dve.memset(fold, 0.0).then_inc(fold_zero, 1)
                table_lo(l, 0, ft_lo[0:FT], ft_raw[0:FT, :].rearrange("p (a b c) -> p a b c", a=2, b=FCH),
                         ft_hi[0:FT], None)
                table_lo(l, 1, cw_lo[:, 0], turn[:, :].rearrange("p (g c) -> p g c", g=FG), cw_hi[:, 0], turn_free)
                table_lo(l, 2, cw_lo[:, 1], mixed[:, :].rearrange("p (g c) -> p g c", g=FG), cw_hi[:, 1], mixed_free)
                with dve.Fori(0, FG - 1) as g:
                    fourier(l, g, T_FOUR + 2 * g, 1, True)
                fourier(l, FG - 1, T_FV3, 1, False)
                with dve.Fori(0, NC) as j:
                    T = T_MIX + 4 * j
                    take(l, T, gf, odd=0)
                    split_lo(l, T + 2, odd=0, n=FG)
                    take(l, T + 1, ga, odd=1)
                    split_lo(l, T + 3, odd=1)
                    for b, g, y in ((0, gf, yf), (1, ga, ya)):
                        dve.wait_ge(m_ready, l * NC + j + 1)
                        dve.wait_ge(tanh_ready, l * HL + H_MIX + 2 * j + b + 1)
                        dve.wait_ge(tile_done, l * TL + T + b + 5)
                        dve.scalar_tensor_tensor(halves(y), halves(g), 1.0, result(b), ALU.add, ALU.mult
                                                 ).then_inc(tile_taken, 1)
                        split_lo(l, T + 4 + b, odd=b)
                def out_tile(j, b):
                    T = T_OUT + 2 * j + b
                    dve.wait_ge(tile_done, l * TL + T + 3)
                    dve.scalar_tensor_tensor(halves(h_t[:, 2 * j + b, :]), result(b), 0.5,
                                             halves(h_t[:, 2 * j + b, :]), ALU.mult, ALU.add).then_inc(tile_taken, 1)
                    dve.wait_ge(tile_taken, l * TL + T + 3)
                    absorb(l * NC + NC + 2 * j + b, l + 1, 2 * j + b, b)

                with dve.Fori(0, NC // 2 - 1) as j:
                    for b in range(2):
                        out_tile(j, b)
                        split_lo(l, T_OUT + 2 + 2 * j + b, odd=b)
                for b in range(2):
                    out_tile(NC // 2 - 1, b)

            dve.wait_ge(x_ready, NC * (DEPTH + 1) + 2)
            dve.wait_ge(hsq_added, NC * (DEPTH + 1) + 2)
            for n in range(2 * ROW_TILES):
                dve.wait_ge(out_turned, n + 1)
                dve.tensor_copy(x_in[:, n // 2, 512 * (n % 2):512 * (n % 2) + 512], acc[:, n % 2, 0, :]
                                ).then_inc(out_ready, 1)

        @block.gpsimd
        def _(pool):
            def minus(dst, a, hi, done):
                pool.tensor_tensor(dst, a, hi.bitcast(F32), ALU.subtract).then_inc(done, 1)

            def absorb(n, c, s, first):
                pool.wait_ge(xh_ready, n + 1)
                minus(x_lo[:, c, :], xg[:, s, :], x_hi[:, c, :], x_ready)
                wait_apart(pool, hsq_ready, n + 1)
                if first:
                    pool.tensor_copy(sqsum[:], hsq[:, s, :]).then_inc(hsq_added, 1)
                else:
                    pool.wait_ge(hsq_added, n + 2)
                    pool.tensor_tensor(sqsum[:], sqsum[:], hsq[:, s, :], ALU.add).then_inc(hsq_added, 1)

            def power(l, r, rows, at, n, exps_at=None):
                pool.wait_ge(ms_ready, l * RL + r + 1)
                if exps_at is not None:
                    pool.wait_ge(score_free, l * WL + exps_at + 2)
                pool.tensor_tensor(rs[0:rows, at:at + n], ms[0:rows, at:at + n], halfneg[0:rows, at:at + n],
                                   ALU.pow).then_inc(rs_ready, 1)

            def rotate(l, unit, table):
                pool.wait_ge(rope_done, l * ROPES + unit + 1)
                pool.wait_ge(swapped, l * 64 * ROPES + 64 * unit + 64)
                pool.tensor_tensor(rp_b, rp_swap, rot[:, table, :], ALU.mult).then_inc(rope_b, 1)
                pool.wait_ge(rope_b, l * ROPES + unit + 1)
                pool.wait_ge(rope_a, l * ROPES + unit + 1)
                pool.tensor_tensor(rp_a, rp_a, rp_b, ALU.add).then_inc(rope_ready, 1)

            def k_lo_part(l, kv, unit):
                pool.wait_ge(rope_hi, l * ROPES + unit + 1)
                minus(k_lo[:, kv, :], rp_b, k_hi[:, kv, :], rope_done)

            def q_lo_part(l, h, unit):
                pool.wait_ge(rope_hi, l * ROPES + unit + 1)
                pool.tensor_tensor(qm_lo[:, h, :], rp_a[:, 0:META], qm_hi[:, h, :].bitcast(F32), ALU.subtract)
                minus(q_lo, rp_a, q_hi, rope_done)

            def normalise(l, q, s, n):
                wait_apart(pool, rinv_ready, l * QTL + q + 1)
                pool.tensor_scalar(prob[0:n, s, :], prob[0:n, s, :], rinv[0:n, s:s + 1], 1.0, ALU.mult,
                                   ALU.mult).then_inc(prob_ready, 1)

            def att_lo_part(l, n, dst, src, hi):
                pool.wait_ge(att_hi_ready, l * ATT + n + 1)
                minus(dst, src, hi, att_done)

            for s, n in ((x_ready, 2), (hsq_added, 2), (rs_ready, 1), (rsq_ready, 1), (rope_ready, 1), (rope_done, 1),
                         (att_done, 1), (fold_ready, 1), (z_ready, 1), (m_ready, 1), (m_done, 1)):
                pool.sem_inc(s, n)
            pool.dma_start(ngain[:, 0:DEPTH, :], norm_g.rearrange("l (c p) -> p l c", p=P)).then_inc(param_in, 16)
            pool.dma_start(bhalf[:], b_gate.rearrange("l (c p) -> p l c", p=P)).then_inc(param_in, 16)
            for n, g in ((0, q_g), (2, k_g)):
                pool.dma_start(gains[:, :, n:n + 1], g.rearrange("l (p o) -> p l o", o=1)).then_inc(param_in, 16)
                for q in range(4):
                    a, b = q * QUARTER, (q ^ 1) * QUARTER
                    pool.dma_start(gains[a:a + QUARTER, :, n + 1:n + 2],
                                   g[:, b:b + QUARTER].rearrange("l (p o) -> p l o", o=1)).then_inc(param_in, 16)
            pool.wait_ge(const_ready, 4)
            for c in range(NC):
                absorb(c, c, c % 2, c == 0)
            with pool.Fori(0, DEPTH) as l:
                power(l, R_H, NT, 0, NP_)
                pool.wait_ge(rot_ready, l + 1)
                rotate(l, 0, 3)
                power(l, R_K0, NT, 0, NP_)
                k_lo_part(l, 0, 0)
                rotate(l, 1, 1)
                q_lo_part(l, 0, 1)
                power(l, R_Q0, P, Q_COL, ROW_TILES)
                rotate(l, 2, 3)
                power(l, R_K1, NT, 0, NP_)
                k_lo_part(l, 1, 2)
                with pool.Fori(0, HEADS - 1) as h:
                    for t in range(4):
                        normalise(l, 4 * h + t, t % 2, P)
                    rotate(l, 3 + h, 1)
                    q_lo_part(l, h + 1, 3 + h)
                    power(l, R_QNEXT + h, P, Q_COL, ROW_TILES, W_HEAD + 4 * h + 3)
                    att_lo_part(l, h, att_lo[:, h, META:S], att[:, META:S], att_hi[:, h, META:S])
                power(l, R_QM, 4 * META, M_COL, KV)
                normalise(l, QT_M0, 0, 4 * META)
                att_lo_part(l, A_M0, att_lo[:, 0:4, 0:META], att[:, 0:4 * META].rearrange("p (a b) -> p a b", a=4),
                            att_hi[:, 0:4, 0:META])
                normalise(l, QT_M0 + 1, 1, 4 * META)
                att_lo_part(l, A_M0 + 1, att_lo[:, 4:8, 0:META], att[:, 0:4 * META].rearrange("p (a b) -> p a b", a=4),
                            att_hi[:, 4:8, 0:META])
                for t in range(4):
                    normalise(l, QT_H7 + t, t % 2, P)
                att_lo_part(l, A_H7, att_lo[:, 7, META:S], att[:, META:S], att_hi[:, 7, META:S])
                with pool.Fori(0, FG) as g:
                    pool.wait_ge(fold_hi_ready, l * FG + g + 1)
                    minus(xf_lo, fold, xf_hi, fold_ready)
                    pool.wait_ge(z_hi_ready, l * FG + g + 2)
                    minus(z_lo[:, g, :], fz, z_hi[:, g, :], z_ready)
                with pool.Fori(0, NC) as j:
                    pool.wait_ge(tile_taken, l * TL + T_MIX + 4 * j + 6)
                    pool.wait_ge(m_done, l * NC + j + 1)
                    pool.tensor_tensor(mm, yf, ya, ALU.add).then_inc(m_ready, 1)
                    pool.wait_ge(m_hi_ready, l * NC + j + 1)
                    minus(m_lo[:, j, :], mm, m_hi[:, j, :], m_done)
                n = l * NC + NC
                absorb(n, 0, 0, True)
                absorb(n + 1, 1, 1, False)
                with pool.Fori(1, NC // 2) as j:
                    for b in range(2):
                        absorb(n + 2 * j + b, 2 * j + b, b, False)


PARAMS = 12


def tables():
    eye = np.eye(P, dtype=np.float32)
    half = HD // 2
    inv = (10000.0 ** (-np.arange(0, half, 2, dtype=np.float32) / np.float32(half))).astype(np.float32)
    t = np.arange(SEQ)
    zero = np.zeros(META, np.float32)
    row = np.concatenate([zero, (t // 64).astype(np.float32)])
    col = np.concatenate([zero, (t % 64).astype(np.float32)])
    ang = [(a[:, None] * inv[None, :]).astype(np.float32).T.astype(np.float64) for a in (row, col)]
    cos = np.concatenate([np.cos(ang[0])] * 2 + [np.cos(ang[1])] * 2)
    sin = np.concatenate([-np.sin(ang[0]), np.sin(ang[0]), -np.sin(ang[1]), np.sin(ang[1])])
    rope = np.stack([cos, sin], axis=1).astype(np.float32)
    tt, ss = np.arange(FT * FCH)[:, None], np.arange(FS)[None, :]
    w = 2 * np.pi * ((tt * ss) % S) / S
    pos = np.stack([np.cos(w), np.sin(w)]).reshape(2, FCH, FT, FS).transpose(2, 0, 1, 3)
    c = np.arange(P)
    v = 2 * np.pi * (np.outer(c, c) % P) / P
    ch = np.concatenate([np.cos(v), np.sin(v)], axis=1) / np.sqrt(S * P)
    return {"eye": eye, "rope": np.ascontiguousarray(rope),
            "dft_pos": np.ascontiguousarray(pos.reshape(FT, 2 * FCH * FS).astype(np.float32)),
            "dft_ch": ch.astype(np.float32)}


INPUTS = ["x", "meta_tokens", "norm_g", "w_in", "b_gate", "q_norm_g", "k_norm_g", "w_fmix", "w_fproj", "w_aproj",
          "w_out"]


def kernel(**inputs):
    import concourse.bacc as bacc
    from concourse.bass_utils import run_bass_kernel_spmd

    nc = bacc.Bacc("TRN2", target_bir_lowering=False, num_devices=1)
    arrays = {"in_" + n: np.ascontiguousarray(inputs[n]) for n in INPUTS}
    arrays.update({"table_" + n: a for n, a in tables().items()})
    args = [nc.dram_tensor(n, a.shape, mybir.dt.from_np(a.dtype), kind="ExternalInput").ap()
            for n, a in arrays.items()]
    out = nc.dram_tensor("out", (1, SEQ, D), F32, kind="ExternalOutput").ap()
    with nc.allow_non_contiguous_dma("gains and biases, a few KB"):
        program(nc, *args, out)
    r = run_bass_kernel_spmd(nc, [arrays], core_ids=[0])
    return r.results[0]["out"]
```

```python
from contextlib import ExitStack

import numpy as np

import concourse.bass as bass
from concourse import mybir

F32, F32R = mybir.dt.float32, mybir.dt.float32r
ALU, ACT, AX = mybir.AluOpType, mybir.ActivationFunctionType, mybir.AxisListType

P = 128
D, SEQ, DEPTH, META = 1024, 512, 2, 16
S = SEQ + META
NC = D // P
HALF = S // 2
HEADS, KV, GQA, HD = 8, 2, 4, 128
FG = 4
ROW_TILES = SEQ // P
KCH = 5
TAIL = 4 * P
NT = 88
NP_ = S // NT
EPS = 1e-6
SCALE = HD ** -0.5
QUARTER = 32
FT, FCH = 89, 3
FS = 266
FOLD = S // 2
assert DEPTH == 2

X_PARTS = ((0, 2), (2, 4), (4, NC))

C_FVAL, C_FGATE, C_Q, C_K, C_V = 0, 512, 1024, 2048, 2304
C_AGATE, C_GF, C_GA = 2560, 3584, 4608

T_K0, T_K1, T_Q0, T_V0, T_V1 = range(5)
T_HEAD = 5
T_FG0 = T_HEAD + 14
T_FOUR = T_HEAD + 16
T_MIX = T_FOUR + 7
T_OUT = T_MIX + 4 * NC
TL = T_OUT + NC

U_RMS, U_K0, U_K1, U_V0, U_Q0, U_V1 = range(6)
U_HEAD = 6
U_M0 = U_HEAD + 5 * HEADS
U_CW = U_M0 + KV
U_A = U_CW + 1
UL = U_A + FG
W_RMS, W_K0, W_K1 = range(3)
W_HEAD = 3
W_M0 = W_HEAD + 4 * HEADS
W_F = W_M0 + KV
WL = W_F + FG
O_V0, O_V1 = range(2)
O_HEAD = 2
O_M0 = O_HEAD + 2 * HEADS
O_SW = O_M0 + 2 * KV
O_B = O_SW + 1
OL = O_B + FG
QT_M0 = 4 * HEADS
QTL = QT_M0 + KV
ROPES = 10
R_H, R_K0, R_K1, R_Q0 = range(4)
R_QM = R_Q0 + HEADS
RL = R_QM + 1
Q_COL, M_COL = 8, 12
NORMS = 3
A_M0 = HEADS
ATT = A_M0 + KV
H_FG, H_MIX, HL = HEADS, HEADS + FG, HEADS + FG + 2 * NC


def program(nc, x, meta, norm_g, w_in, b_gate, q_g, k_g, w_fmix, w_fproj, w_aproj, w_out,
            eye, rope, dft_pos, dft_ch, out):
    with ExitStack() as ctx:
        def sb(name, shape, dt=F32):
            return ctx.enter_context(nc.sbuf_tensor(name, shape, dt))

        def ps(name, shape):
            return ctx.enter_context(nc.psum_tensor(name, shape, F32))

        def sem(name):
            return ctx.enter_context(nc.semaphore(name))

        h_t = sb("h_t", [P, NC, S])
        x_hi, x_lo = sb("x_hi", [P, NC, S], F32R), sb("x_lo", [P, NC, S], F32R)
        w_raw = sb("w_raw", [P, 2, NC, P])
        w_hi, w_lo = sb("w_hi", [P, 2, NC, P], F32R), sb("w_lo", [P, 2, NC, P], F32R)
        att_hi, att_lo = sb("att_hi", [P, NC, S], F32R), sb("att_lo", [P, NC, S], F32R)
        kvz = sb("kvz", [P, 4672], F32R)
        phase = sb("phase", [P, 2 * NC * S], F32R)
        arena = sb("arena", [P, 11 * S])
        rstd = sb("rstd", [P, S])
        rot = sb("rot", [P, 4, S])
        sqsum = sb("sqsum", [P, S])
        fgate = sb("fgate", [P, FG, S])
        ident = sb("ident", [P, P])
        ones = sb("ones", [P, P])
        ngain = sb("ngain", [P, DEPTH + 1, NC])
        bhalf = sb("bhalf", [P, DEPTH, 2 * NC])
        gains = sb("gains", [P, DEPTH, 4])
        ms = sb("ms", [P, 16])
        rs = sb("rs", [P, 16])
        halfneg = sb("halfneg", [P, 16])
        rmax = sb("rmax", [P, 2])
        nbias = sb("nbias", [P, 2])
        rsum = sb("rsum", [P, 2])
        rinv = sb("rinv", [P, 2])
        qm_sq = sb("qm_sq", [P, HEADS, META])
        agm = sb("agm", [P, HEADS, META])

        def region(t, at, *shape):
            n = int(np.prod(shape))
            v = t[:, at:at + n]
            if len(shape) == 2:
                v = v.rearrange("p (a b) -> p a b", a=shape[0])
            if len(shape) == 3:
                v = v.rearrange("p (a b c) -> p a b c", a=shape[0], b=shape[1])
            return v

        k_hi, k_lo = region(kvz, 0, KV, S), region(kvz, KV * S, KV, S)
        v_hi = region(kvz, 2 * KV * S, KV, KCH, P)
        v_lo = region(kvz, 2 * KV * S + KV * KCH * P, KV, KCH, P)
        z_hi, z_lo = region(kvz, 0, FG, S), region(kvz, FG * S, FG, S)
        m_hi, m_lo = region(phase, 0, NC, S), region(phase, NC * S, NC, S)
        pt_hi, pt_lo = region(phase, 0, 4, 4 * P), region(phase, 2048, 4, 4 * P)
        tail_hi, tail_lo = region(phase, 4096, 4 * P), region(phase, 4608, 4 * P)
        q_hi, q_lo = region(phase, 5120, S), region(phase, 5120 + S, S)
        qm_hi, qm_lo = region(phase, 6176, HEADS, META), region(phase, 6304, HEADS, META)
        xf_hi, xf_lo = region(phase, 0, 2, FT * FCH), region(phase, 534, 2, FT * FCH)
        pq_hi, pq_lo = region(phase, 1068, 2 * FCH, P), region(phase, 1836, 2 * FCH, P)
        cw_hi, cw_lo = region(phase, 2604, 2, FG, P), region(phase, 3628, 2, FG, P)
        ft_hi, ft_lo = region(phase, 4652, 2, FCH, FS), region(phase, 6248, 2, FCH, FS)

        def slot(n, k=1):
            return arena[:, n * S:(n + k) * S]

        prob = slot(0, 2).rearrange("p (a b) -> p a b", a=2)
        rp_sq, ag_raw, ag_th, silu, att = slot(4), slot(7), slot(8), slot(9), slot(10)
        diag = slot(10)
        ropes = [[slot(n) for n in (2, 3, 5, 6)], [fgate[:, n, :] for n in range(4)]]
        v_t = slot(7, 2).rearrange("p (a b) -> p a b", a=2)
        def span(at, n):
            return arena[:, at:at + n]

        fv = slot(0)
        fold = span(S, 2 * FT * FCH).rearrange("p (a b) -> p a b", a=2)
        fb, fz = span(1062, FS), span(1328, S)
        ft_raw, ch_raw, fm_raw = span(1856, 2 * FCH * FS), span(3452, 2 * P), span(3708, FG * P)
        gf, ga, yf, ya, mm = slot(4), slot(5), slot(6), slot(7), slot(8)
        hsq, xg = fgate[:, 0:2, :], fgate[:, 2:4, :]
        by_token = region(arena, 0, ROW_TILES, D)
        meta_in = region(arena, ROW_TILES * D, D)

        acc = ps("acc", [P, 2, 2, 512])
        score = ps("score", [P, 2, 512])
        turn = ps("turn", [P, 512])
        mixed = ps("mixed", [P, 512])

        const_in, gain_in, bias_in, param_in = sem("const_in"), sem("gain_in"), sem("bias_in"), sem("param_in")
        x_loaded = [sem(f"x_loaded{n}") for n in range(len(X_PARTS))]
        const_ready = sem("const_ready")
        x_turned = sem("x_turned")
        h_ready, h_ready_odd = sem("h_ready"), sem("h_ready_odd")
        raw_landed = [sem("raw_landed0"), sem("raw_landed1")]
        w_hi_ready = sem("w_hi_ready")
        w_ready = sem("w_ready")
        tile_done = sem("tile_done")
        tile_taken = sem("tile_taken")
        xg_ready, xh_ready = sem("xg_ready"), sem("xh_ready")
        x_ready = sem("x_ready")
        hsq_ready = sem("hsq_ready")
        hsq_added = sem("hsq_added")
        turn_full, turn_free = sem("turn_full"), sem("turn_free")
        score_full, score_free = sem("score_full"), sem("score_free")
        mixed_full, mixed_free = sem("mixed_full"), sem("mixed_free")
        rs_ready = sem("rs_ready")
        diag_ready = sem("diag_ready")
        rot_loaded, rot_ready = sem("rot_loaded"), sem("rot_ready")
        swapped = [sem("swapped0"), sem("swapped1")]
        rsq_ready = sem("rsq_ready")
        rope_parts = sem("rope_parts")
        rope_ready = sem("rope_ready")
        rope_hi = sem("rope_hi")
        rope_done = sem("rope_done")
        v_hi_ready = sem("v_hi_ready")
        max_ready, bias_ready = sem("max_ready"), sem("bias_ready")
        rinv_ready, prob_ready = sem("rinv_ready"), sem("prob_ready")
        pt_hi_ready = sem("pt_hi_ready")
        tail_hi_ready = sem("tail_hi_ready")
        tanh_ready = sem("tanh_ready")
        silu_ready = sem("silu_ready")
        att_hi_ready = sem("att_hi_ready")
        att_done = sem("att_done")
        ft_loaded, ft_hi_ready, ft_ready = sem("ft_loaded"), sem("ft_hi_ready"), sem("ft_ready")
        fold_zero, folded, fold_hi_ready = sem("fold_zero"), sem("folded"), sem("fold_hi_ready")
        fold_ready = sem("fold_ready")
        pq_hi_ready = sem("pq_hi_ready")
        fgate_ready, z_gated = sem("fgate_ready"), sem("z_gated")
        z_hi_ready = sem("z_hi_ready")
        z_ready = sem("z_ready")
        m_hi_ready = sem("m_hi_ready")
        m_done = sem("m_done")
        m_ready = sem("m_ready")
        out_turned, out_stored = sem("out_turned"), sem("out_stored")
        out_ready, out_ready_odd = sem("out_ready"), sem("out_ready_odd")

        waited = sem("waited")

        block = ctx.enter_context(nc.Block())

        def halves(flat):
            return flat.rearrange("p (a b) -> p a b", a=2)

        def flat(t):
            return t.rearrange("p a b -> p (a b)")

        def wait_apart(eng, semaphore, value):
            eng.wait_ge(semaphore, value)
            eng.sem_inc(waited, 1)

        def of_meta(n):
            return isinstance(n, int) and n >= A_M0

        def made(n):
            return att[:, 0:GQA * META].rearrange("p (a b) -> p a b", a=GQA) if of_meta(n) else att[:, META:S]

        def place(t, n):
            a = GQA * (n - A_M0) if of_meta(n) else n
            return t[:, a:a + GQA, 0:META] if of_meta(n) else t[:, n, META:S]

        def by_dve(c):
            return c + 1 + c // 2 + 1

        def slot_of(T, odd):
            return T % 2 if odd is None else odd

        @block.sync
        def _(sp):
            sp.dma_start(ident[:], eye).then_inc(const_in, 16)
            for n, chunks in enumerate(X_PARTS):
                a = slice(chunks[0] * P, chunks[1] * P)
                for t in range(ROW_TILES):
                    sp.dma_start(by_token[:, t, a], x[0, t * P:(t + 1) * P, a]).then_inc(x_loaded[n], 16)
                sp.dma_start(meta_in[0:META, a], meta[:, a]).then_inc(x_loaded[n], 16)

            def load(l, T, w, col, odd=None, rows=D, of=None):
                of = l if of is None else of
                s = slot_of(T, odd)
                wait_apart(sp, w_ready, l * TL + T + 1)
                sp.dma_start(w_raw[:, s, 0:rows // P, :],
                             w[of, :, bass.ds(col, P)].rearrange("(k p) f -> p k f", p=P)
                             ).then_inc(raw_landed[s], 16)

            def swap(l, T, unit, rp=0):
                raw, partner = ropes[rp][0], ropes[rp][1]
                wait_apart(sp, tile_taken, l * TL + T + 3)
                if not rp:
                    wait_apart(sp, rope_ready, l * ROPES + unit + 1)
                for q in range(4):
                    a, b = q * QUARTER, (q ^ 1) * QUARTER
                    sp.dma_start(partner[a:a + QUARTER, :], raw[b:b + QUARTER, :]).then_inc(swapped[rp], 16)

            load(0, T_K0, w_in, C_K)
            load(0, T_K1, w_in, C_K + P)
            with sp.Fori(0, DEPTH) as l:
                load(l, T_Q0, w_in, C_Q)
                wait_apart(sp, rope_done, l * ROPES + 1)
                sp.dma_start(rot[:, 0:2, :], rope).then_inc(rot_loaded, 16)
                sp.dma_start(rot[:, 2:4, :], rope).then_inc(rot_loaded, 16)
                load(l, T_V0, w_in, C_V)
                load(l, T_V1, w_in, C_V + P)
                swap(l, T_K0, 0)
                swap(l, T_K1, 1, 1)
                load(l, T_HEAD, w_in, C_Q + P)
                swap(l, T_Q0, 2)
                load(l, T_HEAD + 1, w_in, C_AGATE)
                load(l, T_HEAD + 2, w_in, C_Q + 2 * P)
                with sp.Fori(0, HEADS - 3) as h:
                    load(l, T_HEAD + 3 + 2 * h, w_in, C_AGATE + P + P * h, odd=0)
                    swap(l, T_HEAD + 2 * h, 3 + h)
                    load(l, T_HEAD + 4 + 2 * h, w_in, C_Q + 3 * P + P * h, odd=1)
                load(l, T_HEAD + 13, w_in, C_AGATE + 6 * P)
                swap(l, T_HEAD + 10, 8)
                load(l, T_FG0, w_in, C_FGATE)
                load(l, T_FG0 + 1, w_in, C_AGATE + 7 * P)
                swap(l, T_HEAD + 12, 9)
                load(l, T_FOUR, w_in, C_FVAL)
                load(l, T_FOUR + 1, w_in, C_FGATE + P)
                wait_apart(sp, rope_done, l * ROPES + ROPES + 1)
                wait_apart(sp, turn_full, l * UL + U_HEAD + 5 * 6 + 5)
                sp.dma_start(ft_raw[0:FT, :], dft_pos).then_inc(ft_loaded, 16)
                wait_apart(sp, silu_ready, l * HEADS + HEADS)
                sp.dma_start(ch_raw, dft_ch).then_inc(ft_loaded, 16)
                sp.dma_start(fm_raw.rearrange("p (g c) -> p g c", g=FG),
                             w_fmix[l].rearrange("g d c -> d g c")).then_inc(ft_loaded, 16)
                load(l, T_FOUR + 2, w_in, C_FVAL + P)
                load(l, T_FOUR + 3, w_in, C_FGATE + 2 * P)
                load(l, T_FOUR + 4, w_in, C_FVAL + 2 * P)
                load(l, T_FOUR + 5, w_in, C_FGATE + 3 * P)
                load(l, T_FOUR + 6, w_in, C_FVAL + 3 * P)
                with sp.Fori(0, NC) as j:
                    load(l, T_MIX + 4 * j, w_in, C_GF + P * j, odd=0)
                    load(l, T_MIX + 1 + 4 * j, w_in, C_GA + P * j, odd=1)
                    load(l, T_MIX + 2 + 4 * j, w_aproj, P * j, odd=0)
                    load(l, T_MIX + 3 + 4 * j, w_fproj, P * j, odd=1, rows=FG * P)
                with sp.Fori(0, NC // 2) as j:
                    load(l, T_OUT + 2 * j, w_out, 2 * P * j, odd=0)
                    load(l, T_OUT + 1 + 2 * j, w_out, P + 2 * P * j, odd=1)
                load(l, TL, w_in, C_K, of=DEPTH - 1 - l)
                load(l, TL + 1, w_in, C_K + P, of=DEPTH - 1 - l)
            for t in range(ROW_TILES):
                for half, ready in enumerate((out_ready, out_ready_odd)):
                    a = slice(half * D // 2, (half + 1) * D // 2)
                    sp.wait_ge(ready, t + 1)
                    sp.dma_start(out[0, t * P:(t + 1) * P, a], by_token[:, t, a]).then_inc(out_stored, 16)
            sp.wait_ge(out_stored, 32 * ROW_TILES)

        @block.tensor
        def _(pe):
            def passes(dst, whi, wlo, mhi, mlo, first, last, done=None):
                for n, (w, m) in enumerate(((wlo, mhi), (whi, mlo), (whi, mhi))):
                    for b in range(len(dst)):
                        i = pe.matmul(dst[b], w, m[b], start=first and n == 0, stop=last and n == 2)
                if done is not None:
                    i.then_inc(done, 1)

            def cols(t):
                return [t[:, 0:HALF], t[:, HALF:S]]

            def tile(l, T, k0=0, k1=NC, odd=None, hi=x_hi, lo=x_lo, chunks=NC, ahead=None):
                s = slot_of(T, odd)
                if k0 == 0:
                    pe.wait_ge(w_ready, l * TL + T + 3)
                    pe.wait_ge(tile_taken, l * TL + T + 1)
                for k in range(k0, min(k1, chunks)):
                    if ahead is not None:
                        ahead(k)
                    passes([acc[:, s, 0, 0:HALF], acc[:, s, 1, 0:HALF]], w_hi[:, s, k, :], w_lo[:, s, k, :],
                           cols(hi[:, k, :]), cols(lo[:, k, :]), k == 0, k == chunks - 1,
                           tile_done if k == chunks - 1 else None)

            def sum_squares(l, use, src):
                pe.wait_ge(turn_free, l * UL + use + 1)
                for t in range(NP_):
                    i = pe.matmul(turn[0:NT, t:t + 1], src[:, NT * t:NT * (t + 1)], ones[:, 0:1],
                                  start=True, stop=True)
                i.then_inc(turn_full, 1)

            def broadcast(l, n, use):
                pe.wait_ge(diag_ready, l * NORMS + n + 1)
                pe.wait_ge(score_free, l * WL + use + 1)
                for b in range(2):
                    i = pe.matmul(score[:, b, 0:HALF], ones[0:NT, :], diag[0:NT, HALF * b:HALF * (b + 1)],
                                  start=True, stop=True)
                i.then_inc(score_full, 1)

            def turn_values(l, kv):
                pe.wait_ge(tile_taken, l * TL + T_V0 + kv + 3)
                pe.wait_ge(turn_free, l * UL + (U_V0, U_V1)[kv] + 1)
                pe.wait_ge(mixed_free, l * OL + O_V0 + kv + 1)
                for c in range(4):
                    i = pe.transpose(turn[:, c * P:(c + 1) * P], v_t[:, kv, c * P:(c + 1) * P], ident[:])
                i.then_inc(turn_full, 1)
                pe.transpose(mixed[0:META, 0:P], v_t[:, kv, TAIL:S], ident[:]).then_inc(mixed_full, 1)

            def q_norm(l, use, unit):
                pe.wait_ge(rsq_ready, l * ROPES + unit + 2)
                pe.wait_ge(turn_free, l * UL + use + 1)
                for t in range(ROW_TILES):
                    i = pe.matmul(turn[:, t:t + 1], rp_sq[:, META + P * t:META + P * (t + 1)], ones[:, 0:1],
                                  start=True, stop=True)
                i.then_inc(turn_full, 1)

            def scores(l, use, qhi, qlo, kv, n):
                pe.wait_ge(score_free, l * WL + use + 1)
                passes([score[0:n, 0, 0:HALF], score[0:n, 1, 0:HALF]], qhi, qlo,
                       cols(k_hi[:, kv, :]), cols(k_lo[:, kv, :]), True, True, score_full)

            def turn_probs(l, q, use, s, n, tail_at, tail_last):
                pe.wait_ge(turn_free, l * UL + use + 1)
                wait_apart(pe, prob_ready, l * QTL + q + 1)
                i = pe.transpose(mixed[0:META, tail_at:tail_at + n], prob[0:n, s, TAIL:S], ident[0:n, 0:n])
                if tail_last:
                    i.then_inc(mixed_full, 1)
                for c in range(4):
                    i = pe.transpose(turn[:, c * n:(c + 1) * n], prob[0:n, s, c * P:(c + 1) * P], ident[0:n, 0:n])
                i.then_inc(turn_full, 1)

            def weigh_values(l, use, last_use, kv, n):
                pe.wait_ge(turn_free, l * UL + last_use + 2)
                pe.wait_ge(mixed_free, l * OL + use + 1)
                for c in range(KCH):
                    rows = P if c < 4 else META
                    hi = pt_hi[:, c, 0:n] if c < 4 else tail_hi[0:META, 0:n]
                    lo = pt_lo[:, c, 0:n] if c < 4 else tail_lo[0:META, 0:n]
                    passes([mixed[:, 0:n]], v_hi[0:rows, kv, c, :], v_lo[0:rows, kv, c, :], [hi], [lo],
                           c == 0, c == KCH - 1, mixed_full if c == KCH - 1 else None)

            def query(l, w, t, kv):
                a = META + P * t
                scores(l, w + t, q_hi[:, a:a + P], q_lo[:, a:a + P], kv, P)

            def turned(l, q, u, o, t):
                if t == 0:
                    pe.wait_ge(mixed_free, l * OL + o + 1)
                turn_probs(l, q + t, u + t, t % 2, P, P * t, t == 3)

            def head(l, h, kv, last=False):
                A, B = T_HEAD + 2 * h, T_HEAD + 1 + 2 * h
                u, w, o, q = U_HEAD + 5 * h, W_HEAD + 4 * h, O_HEAD + 2 * h, 4 * h
                pe.wait_ge(rope_done, l * ROPES + h + 4)
                query(l, w, 0, kv)
                tile(l, A, 0, 3, odd=1)
                query(l, w, 1, kv)
                turned(l, q, u, o, 0)
                tile(l, A, 3, 6, odd=1)
                query(l, w, 2, kv)
                turned(l, q, u, o, 1)
                tile(l, A, 6, NC, odd=1)
                tile(l, B, 0, 1, odd=0)
                query(l, w, 3, kv)
                turned(l, q, u, o, 2)
                tile(l, B, 1, 5, odd=0)
                turned(l, q, u, o, 3)
                tile(l, B, 5, NC, odd=0)
                if last:
                    pe.wait_ge(turn_free, l * UL + u + 5)
                    for kv_of in range(KV):
                        i = pe.matmul(turn[0:4 * META, kv_of:kv_of + 1], flat(qm_sq[:, 4 * kv_of:4 * kv_of + 4, :]),
                                      ones[:, 0:1], start=True, stop=True)
                    i.then_inc(turn_full, 1)
                else:
                    q_norm(l, u + 4, 3 + h)
                weigh_values(l, o + 1, u + 3, kv, 4 * P)

            def meta_query(l, kv):
                scores(l, W_M0 + kv, flat(qm_hi[:, 4 * kv:4 * kv + 4, :]), flat(qm_lo[:, 4 * kv:4 * kv + 4, :]),
                       kv, 4 * META)

            def turned_meta(l, kv):
                pe.wait_ge(mixed_free, l * OL + O_M0 + 2 * kv + 1)
                turn_probs(l, QT_M0 + kv, U_M0 + kv, kv, 4 * META, 0, True)

            def channels(l, g):
                pe.wait_ge(fold_ready, l * FG + g + 2)
                pe.wait_ge(score_free, l * WL + W_F + g + 1)
                for part in range(2):
                    for c in range(FCH):
                        a = slice(FT * c, FT * (c + 1))
                        passes([score[0:FT, part, P * c:P * (c + 1)]], xf_hi[:, part, a], xf_lo[:, part, a],
                               [cw_hi[:, part, g, :]], [cw_lo[:, part, g, :]], True, True,
                               score_full if part and c == FCH - 1 else None)

            def positions(l, g):
                pe.wait_ge(score_free, l * WL + W_F + g + 2)
                pe.wait_ge(ft_ready, l + 1)
                for part, (bank, free, full, use) in enumerate(((turn, turn_free, turn_full, l * UL + U_A),
                                                               (mixed, mixed_free, mixed_full, l * OL + O_B))):
                    pe.wait_ge(free, use + g + 1)
                    for c in range(FCH):
                        r = part * FCH + c
                        passes([bank[:, 0:FS]], pq_hi[0:FT, r, :], pq_lo[0:FT, r, :],
                               [ft_hi[0:FT, part, c, :]], [ft_lo[0:FT, part, c, :]], c == 0, c == FCH - 1,
                               full if c == FCH - 1 else None)

            pe.sem_inc(tile_done, 2)
            pe.wait_ge(const_in, 16)
            for c in range(NC):
                for n, chunks in enumerate(X_PARTS):
                    if c == chunks[0]:
                        pe.wait_ge(x_loaded[n], 16 * (ROW_TILES + 1))
                if c >= 2:
                    pe.wait_ge(h_ready, by_dve(c - 2))
                if c >= 3:
                    pe.wait_ge(h_ready_odd, (c - 1) // 2)
                main, rest = (score[:, 0, :], score[:, 1, :]) if c % 2 == 0 else (turn, mixed)
                for t in range(ROW_TILES):
                    pe.transpose(main[:, t * P:(t + 1) * P], by_token[:, t, c * P:(c + 1) * P], ident[:])
                pe.transpose(rest[:, 0:META], meta_in[0:META, c * P:(c + 1) * P], ident[0:META, 0:META]
                             ).then_inc(x_turned, 1)
            pe.wait_ge(const_ready, 3)

            with pe.Fori(0, DEPTH) as l:
                def x_chunk(k):
                    pe.wait_ge(x_ready, l * NC + k + 3)
                tile(l, T_K0, ahead=x_chunk)
                pe.wait_ge(h_ready, by_dve(NC - 1))
                pe.wait_ge(h_ready_odd, NC // 2)
                pe.wait_ge(hsq_added, l * NC + NC + 2)
                sum_squares(l, U_RMS, sqsum)
                tile(l, T_K1, 0, 4)
                broadcast(l, 0, W_RMS)
                tile(l, T_K1, 4, NC)
                tile(l, T_Q0, 0, 4)
                pe.wait_ge(rsq_ready, l * ROPES + 2)
                sum_squares(l, U_K0, rp_sq)
                tile(l, T_Q0, 4, NC)
                pe.wait_ge(rsq_ready, l * ROPES + 3)
                sum_squares(l, U_K1, silu)
                tile(l, T_V0, 0, 4)
                broadcast(l, 1, W_K0)
                tile(l, T_V0, 4, NC)
                broadcast(l, 2, W_K1)
                tile(l, T_V1, 0, 5)
                turn_values(l, 0)
                tile(l, T_V1, 5, NC)
                q_norm(l, U_Q0, 2)
                turn_values(l, 1)
                with pe.Fori(0, GQA) as h:
                    head(l, h, 0)
                with pe.Fori(GQA, HEADS - 1) as h:
                    head(l, h, 1)
                head(l, HEADS - 1, 1, True)
                meta_query(l, 0)
                tile(l, T_FOUR, 0, 3)
                meta_query(l, 1)
                tile(l, T_FOUR, 3, 4)
                turned_meta(l, 0)
                tile(l, T_FOUR, 4, 6)
                weigh_values(l, O_M0 + 1, U_M0, 0, 4 * META)
                tile(l, T_FOUR, 6, NC)
                turned_meta(l, 1)
                tile(l, T_FOUR + 1, 0, 2)
                weigh_values(l, O_M0 + 3, U_M0 + 1, 1, 4 * META)

                pe.wait_ge(ft_loaded, l * 48 + 48)
                pe.wait_ge(turn_free, l * UL + U_CW + 1)
                pe.matmul(turn[:, :], ch_raw[:, 0:P], fm_raw, start=True, stop=True).then_inc(turn_full, 1)
                tile(l, T_FOUR + 1, 2, 3)
                pe.wait_ge(mixed_free, l * OL + O_SW + 1)
                pe.matmul(mixed[:, :], ch_raw[:, P:2 * P], fm_raw, start=True, stop=True).then_inc(mixed_full, 1)
                tile(l, T_FOUR + 1, 3, NC)
                pe.wait_ge(turn_free, l * UL + U_CW + 2)
                pe.wait_ge(mixed_free, l * OL + O_SW + 2)
                channels(l, 0)
                with pe.Fori(1, FG - 1) as g:
                    tile(l, T_FOUR + 2 * g, 0, 3, odd=1)
                    positions(l, g - 1)
                    tile(l, T_FOUR + 2 * g, 3, NC, odd=1)
                    tile(l, T_FOUR + 1 + 2 * g, odd=0)
                    channels(l, g)
                tile(l, T_FOUR + 6, 0, 3)
                positions(l, FG - 2)
                tile(l, T_FOUR + 6, 3, NC)

                def mix(j):
                    tile(l, T_MIX + 2 + 4 * j, odd=0, hi=att_hi, lo=att_lo)
                    pe.wait_ge(z_ready, l * FG + FG + 1)
                    tile(l, T_MIX + 3 + 4 * j, odd=1, hi=z_hi, lo=z_lo, chunks=FG)
                tile(l, T_MIX)
                channels(l, FG - 1)
                tile(l, T_MIX + 1, 0, 4)
                positions(l, FG - 1)
                tile(l, T_MIX + 1, 4, NC)
                wait_apart(pe, att_done, l * ATT + ATT + 1)
                mix(0)
                with pe.Fori(1, NC) as j:
                    tile(l, T_MIX + 4 * j, odd=0)
                    tile(l, T_MIX + 1 + 4 * j, odd=1)
                    mix(j)
                with pe.Fori(0, NC // 2) as j:
                    tile(l, T_OUT + 2 * j, odd=0, hi=m_hi, lo=m_lo,
                         ahead=lambda k: pe.wait_ge(m_done, l * NC + k + 2))
                    tile(l, T_OUT + 1 + 2 * j, odd=1, hi=m_hi, lo=m_lo)

            pe.wait_ge(tile_taken, DEPTH * TL + 2)
            for n in range(2 * ROW_TILES):
                t, half = n // 2, n % 2
                if t >= 2:
                    pe.wait_ge(out_ready_odd if half else out_ready, t - 1)
                for c in range(4):
                    i = pe.transpose(acc[:, t % 2, half, c * P:(c + 1) * P],
                                     h_t[:, 4 * half + c, META + t * P:META + (t + 1) * P], ident[:])
                i.then_inc(out_turned, 1)

        @block.scalar
        def _(act):
            def split_hi(l, T, odd=None, n=NC):
                s = slot_of(T, odd)
                act.wait_ge(raw_landed[s], 8 * TL * l + 8 * (T - s) + 16)
                act.wait_ge(tile_done, l * TL + T + 1)
                act.activation(w_hi[:, s, 0:n, :], w_raw[:, s, 0:n, :], ACT.Copy).then_inc(w_hi_ready, 1)

            def absorb(n, c, s):
                act.wait_ge(xg_ready, n + 1)
                act.activation(x_hi[:, c, :], xg[:, s, :], ACT.Copy).then_inc(xh_ready, 1)
                act.wait_ge(hsq_added, n + 1)
                act.activation(hsq[:, s, :], h_t[:, c, :], ACT.Square).then_inc(hsq_ready, 1)

            def square(l, T, norm_use, rp=0):
                act.wait_ge(turn_full, l * UL + norm_use + 1)
                act.wait_ge(tile_taken, l * TL + T + 3)
                act.activation(silu if rp else rp_sq, ropes[rp][0], ACT.Square).then_inc(rsq_ready, 1)

            def q_square(l, T, norm_use, h):
                act.wait_ge(tile_taken, l * TL + T + 3)
                act.activation(qm_sq[:, h, :], ropes[0][0][:, 0:META], ACT.Square)
                square(l, T, norm_use)

            def k_hi_part(l, kv):
                act.wait_ge(score_free, l * WL + W_K0 + kv + 2)
                act.activation(k_hi[:, kv, :], ropes[kv][3], ACT.Copy).then_inc(rope_hi, 1)

            def q_hi_part(l, h, unit):
                act.wait_ge(rope_ready, l * ROPES + unit + 2)
                act.activation(qm_hi[:, h, :], ropes[0][2][:, 0:META], ACT.Copy)
                act.activation(q_hi, ropes[0][2], ACT.Copy).then_inc(rope_hi, 1)

            def value_hi(l, kv):
                act.wait_ge(turn_full, l * UL + (U_V0, U_V1)[kv] + 1)
                act.wait_ge(mixed_full, l * OL + O_V0 + kv + 1)
                act.activation(v_hi[0:META, kv, 4, :], mixed[0:META, 0:P], ACT.Copy)
                act.activation(v_hi[:, kv, 0:4, :], turn[:, :].rearrange("p (c d) -> p c d", c=4),
                               ACT.Copy).then_inc(v_hi_ready, 1)

            def exps(l, q, s, n, col, slot_use):
                act.wait_ge(turn_full, l * UL + slot_use + 1)
                act.wait_ge(bias_ready, l * QTL + q + 1)
                act.activation(halves(prob[0:n, s, :]), score[0:n, :, 0:HALF], ACT.Exp, bias=nbias[0:n, s:s + 1],
                               scale=rs[0:n, col:col + 1], accum_out=rsum[0:n, s:s + 1]).then_inc(score_free, 1)

            def probs_hi(l, use, n, at, o):
                act.wait_ge(mixed_full, l * OL + o)
                act.wait_ge(turn_full, l * UL + use + 1)
                act.activation(pt_hi[:, :, at:at + n], turn[:, 0:4 * n].rearrange("p (c q) -> p c q", c=4),
                               ACT.Copy).then_inc(pt_hi_ready, 1)

            def tail_hi_part(l, o, n):
                act.wait_ge(mixed_full, l * OL + o + 1)
                act.activation(tail_hi[0:META, 0:n], mixed[0:META, 0:n], ACT.Copy).then_inc(tail_hi_ready, 1)

            def gate_tanh(l, T, src):
                act.wait_ge(tile_taken, l * TL + T + 3)
                act.activation(ag_th, src, ACT.Tanh, scale=0.5).then_inc(tanh_ready, 1)

            def att_hi_part(l, n, o):
                act.wait_ge(mixed_free, l * OL + o + 2)
                act.activation(place(att_hi, n), made(n), ACT.Copy).then_inc(att_hi_ready, 1)

            def meta_exps(l, kv):
                exps(l, QT_M0 + kv, kv, 4 * META, M_COL + kv, U_M0 - 3 + kv)

            def meta_probs_hi(l, kv):
                probs_hi(l, U_M0 + kv, 4 * META, 0, O_M0 + 2 * kv)
                tail_hi_part(l, O_M0 + 2 * kv, 4 * META)

            def head(l, h, last=False):
                u, o, q = U_HEAD + 5 * h, O_HEAD + 2 * h, 4 * h
                exps(l, q, 0, P, Q_COL, u - 3)
                probs_hi(l, u, P, 0, o)
                exps(l, q + 1, 1, P, Q_COL + 1, u - 2)
                probs_hi(l, u + 1, P, P, o)
                exps(l, q + 2, 0, P, Q_COL + 2, u)
                if not last:
                    q_square(l, T_HEAD + 2 * h, u - 1, h + 1)
                probs_hi(l, u + 2, P, 2 * P, o)
                exps(l, q + 3, 1, P, Q_COL + 3, u + 1)
                split_hi(l, T_HEAD + 2 + 2 * h, odd=1)
                tail_hi_part(l, o, 4 * P)
                probs_hi(l, u + 3, P, 3 * P, o)
                if not last:
                    q_hi_part(l, h + 1, 3 + h)
                gate_tanh(l, T_HEAD + 1 + 2 * h, ag_raw)
                split_hi(l, T_HEAD + 3 + 2 * h, odd=0)
                att_hi_part(l, h, o + 1)

            def fold_hi_part(l, g):
                act.wait_ge(score_full, l * WL + W_F + g)
                act.wait_ge(folded, l * FG + g + 1)
                act.activation(xf_hi, fold, ACT.Copy).then_inc(fold_hi_ready, 1)

            def channels_hi_part(l, g):
                act.wait_ge(mixed_full, l * OL + O_B + g)
                act.wait_ge(score_full, l * WL + W_F + g + 1)
                act.activation(pq_hi[0:FT, :, :].rearrange("p (a c) n -> p a (c n)", a=2), score[0:FT, :, 0:FCH * P],
                               ACT.Copy).then_inc(pq_hi_ready, 1)

            def sines(l, g):
                act.wait_ge(z_hi_ready, l * FG + g + 1)
                act.wait_ge(mixed_full, l * OL + O_B + g + 1)
                act.activation(fb[:, 0:FOLD + 1], mixed[:, 0:FOLD + 1], ACT.Copy).then_inc(mixed_free, 1)

            def z_hi_part(l, g):
                act.wait_ge(z_gated, l * FG + g + 1)
                act.activation(z_hi[:, g, :], fz, ACT.Copy).then_inc(z_hi_ready, 1)

            def gate_of_mix(l, j, b):
                g = ga if b else gf
                act.wait_ge(tile_taken, l * TL + T_MIX + 4 * j + b + 3)
                act.activation(g, g, ACT.Tanh, scale=0.5,
                               bias=bhalf[:, l, bass.ds(NC * b + j, 1)]).then_inc(tanh_ready, 1)

            def mix(l, j):
                T = T_MIX + 4 * j
                split_hi(l, T + 4, odd=0)
                split_hi(l, T + 5, odd=1)
                act.wait_ge(m_ready, l * NC + j + 2)
                act.activation(m_hi[:, j, :], mm, ACT.Copy).then_inc(m_hi_ready, 1)

            for n, g in ((0, q_g), (2, k_g)):
                act.dma_start(gains[:, :, n:n + 1], g.rearrange("l (p o) -> p l o", o=1)).then_inc(param_in, 16)
                for q in range(4):
                    a, b = q * QUARTER, (q ^ 1) * QUARTER
                    act.dma_start(gains[a:a + QUARTER, :, n + 1:n + 2],
                                  g[:, b:b + QUARTER].rearrange("l (p o) -> p l o", o=1)).then_inc(param_in, 16)
            act.sem_inc(z_hi_ready, 1)
            for c in range(NC):
                if c % 2 == 0:
                    act.wait_ge(x_turned, c + 2)
                    act.activation(h_t[:, c + 1, META:S], turn[:, 0:SEQ], ACT.Copy).then_inc(h_ready_odd, 1)
                absorb(c, c, c % 2)
                if c == 3 or c == NC - 1:
                    split_hi(0, T_K0 + c // 4)
            with act.Fori(0, DEPTH) as l:
                split_hi(l, T_Q0)
                square(l, T_K0, U_RMS)
                split_hi(l, T_V0)
                square(l, T_K1, U_RMS, 1)
                split_hi(l, T_V1)
                q_square(l, T_Q0, U_K0, 0)
                k_hi_part(l, 0)
                split_hi(l, T_HEAD)
                q_hi_part(l, 0, 2)
                k_hi_part(l, 1)
                value_hi(l, 0)
                split_hi(l, T_HEAD + 1)
                value_hi(l, 1)
                with act.Fori(0, HEADS - 1) as h:
                    head(l, h)
                head(l, HEADS - 1, True)
                meta_exps(l, 0)
                meta_probs_hi(l, 0)
                meta_exps(l, 1)
                gate_tanh(l, T_FG0, fgate[:, 0, :])
                att_hi_part(l, A_M0, O_M0 + 1)
                meta_probs_hi(l, 1)
                split_hi(l, T_FOUR + 2)
                att_hi_part(l, A_M0 + 1, O_M0 + 3)
                fold_hi_part(l, 0)
                act.wait_ge(turn_full, l * UL + U_CW + 1)
                act.activation(cw_hi[:, 0], turn[:, :].rearrange("p (g c) -> p g c", g=FG),
                               ACT.Copy).then_inc(ft_hi_ready, 1)
                act.wait_ge(mixed_full, l * OL + O_SW + 1)
                act.activation(cw_hi[:, 1], mixed[:, :].rearrange("p (g c) -> p g c", g=FG),
                               ACT.Copy).then_inc(ft_hi_ready, 1)
                act.wait_ge(ft_loaded, l * 48 + 48)
                act.activation(ft_hi[0:FT], ft_raw[0:FT, :].rearrange("p (a b c) -> p a b c", a=2, b=FCH),
                               ACT.Copy).then_inc(ft_hi_ready, 1)
                split_hi(l, T_FOUR + 3)
                channels_hi_part(l, 0)
                gate_tanh(l, T_FOUR + 1, fgate[:, 1, :])
                with act.Fori(1, FG - 1) as g:
                    sines(l, g - 1)
                    z_hi_part(l, g - 1)
                    split_hi(l, T_FOUR + 2 + 2 * g, odd=1)
                    fold_hi_part(l, g)
                    split_hi(l, T_FOUR + 3 + 2 * g, odd=0)
                    channels_hi_part(l, g)
                    gate_tanh(l, T_FOUR + 1 + 2 * g, fgate[:, g + 1, :])
                sines(l, FG - 2)
                z_hi_part(l, FG - 2)
                split_hi(l, T_MIX + 1)
                fold_hi_part(l, FG - 1)
                split_hi(l, T_MIX + 2)
                channels_hi_part(l, FG - 1)
                gate_of_mix(l, 0, 0)
                sines(l, FG - 1)
                z_hi_part(l, FG - 1)
                split_hi(l, T_MIX + 3, n=FG)
                gate_of_mix(l, 0, 1)
                mix(l, 0)
                with act.Fori(1, NC) as j:
                    split_hi(l, T_MIX + 2 + 4 * j, odd=0)
                    gate_of_mix(l, j, 0)
                    split_hi(l, T_MIX + 3 + 4 * j, odd=1, n=FG)
                    gate_of_mix(l, j, 1)
                    mix(l, j)
                with act.Fori(0, NC // 2) as j:
                    for b in range(2):
                        split_hi(l, T_OUT + 2 + 2 * j + b, odd=b)
                        absorb(l * NC + NC + 2 * j + b, 2 * j + b, b)
            for t in range(ROW_TILES):
                act.wait_ge(out_turned, 2 * t + 2)
                act.activation(by_token[:, t, D // 2:D], acc[:, t % 2, 1, :], ACT.Copy).then_inc(out_ready_odd, 1)

        @block.vector
        def _(dve):
            def split_lo(l, T, odd=None, n=NC):
                s = slot_of(T, odd)
                dve.wait_ge(w_hi_ready, l * TL + T + 1)
                dve.tensor_tensor(w_lo[:, s, 0:n, :], w_raw[:, s, 0:n, :], w_hi[:, s, 0:n, :].bitcast(F32),
                                  ALU.subtract).then_inc(w_ready, 1)

            def result(s):
                return acc[:, s, :, 0:HALF]

            def take(l, T, dst, odd=None):
                dve.wait_ge(tile_done, l * TL + T + 3)
                dve.tensor_tensor(halves(dst), result(slot_of(T, odd)), halves(rstd[:]), ALU.mult
                                  ).then_inc(tile_taken, 1)

            def take_rope(l, T, unit, odd=None, rp=0):
                if not rp:
                    dve.wait_ge(rsq_ready, l * ROPES + unit + 1)
                    dve.wait_ge(rope_ready, l * ROPES + unit + 1)
                take(l, T, ropes[rp][0], odd)

            def absorb(n, gain_l, c, s):
                dve.wait_ge(x_ready, n + 1)
                dve.tensor_scalar(xg[:, s, :], h_t[:, c, :], ngain[:, gain_l, bass.ds(c, 1)], None,
                                  ALU.mult).then_inc(xg_ready, 1)

            def mean_squares(l, use, r, rows, at, n, scale, eps):
                dve.wait_ge(rs_ready, l * RL + r + 1)
                dve.wait_ge(turn_full, l * UL + use + 1)
                dve.tensor_scalar(ms[0:rows, at:at + n], turn[0:rows, 0:n], scale, eps, ALU.mult, ALU.add
                                  ).then_inc(turn_free, 1)

            def diagonals(l, r, n):
                dve.wait_ge(rs_ready, l * RL + r + 2)
                shape = [NT, NP_, NT]
                dve.tensor_tensor(diag[0:NT, :].rearrange("p (a b) -> p a b", a=NP_),
                                  ident[0:NT, 0:NT].unsqueeze(1).broadcast_to(shape),
                                  rs[0:NT, 0:NP_].unsqueeze(2).broadcast_to(shape), ALU.mult).then_inc(diag_ready, 1)

            def rotate_cos(l, unit, table, T, rp=0, split=None):
                if split is not None:
                    dve.wait_ge(rope_done, l * ROPES + split + 1)
                dve.wait_ge(tile_taken, l * TL + T + 3)
                dve.tensor_tensor(ropes[rp][2], ropes[rp][0], rot[:, table, :], ALU.mult).then_inc(rope_parts, 1)

            def rotate_sin(l, unit, table, before, rp=0):
                dve.wait_ge(swapped[rp], 64 * before + 64)
                dve.tensor_tensor(ropes[rp][3], ropes[rp][1], rot[:, table + 1, :], ALU.mult).then_inc(rope_parts, 1)
                dve.wait_ge(rope_parts, l * 2 * ROPES + 2 * unit + 2)
                dve.tensor_tensor(ropes[rp][2], ropes[rp][2], ropes[rp][3], ALU.add).then_inc(rope_ready, 1)

            def rotate(l, unit, table, before, T, rp=0, split=None):
                rotate_cos(l, unit, table, T, rp, split)
                rotate_sin(l, unit, table, before, rp)

            def scale_k(l, kv):
                dve.wait_ge(rope_ready, l * ROPES + kv + 2)
                dve.wait_ge(score_full, l * WL + W_K0 + kv + 1)
                dve.tensor_tensor(halves(ropes[kv][3]), score[:, :, 0:HALF], halves(ropes[kv][2]), ALU.mult
                                  ).then_inc(score_free, 1)

            def value_lo(l, kv):
                dve.wait_ge(v_hi_ready, l * KV + kv + 1)
                dve.tensor_tensor(v_lo[0:META, kv, 4, :], mixed[0:META, 0:P], v_hi[0:META, kv, 4, :].bitcast(F32),
                                  ALU.subtract).then_inc(mixed_free, 1)
                dve.tensor_tensor(v_lo[:, kv, 0:4, :], turn[:, :].rearrange("p (c d) -> p c d", c=4),
                                  v_hi[:, kv, 0:4, :].bitcast(F32), ALU.subtract).then_inc(turn_free, 1)

            def maximum(l, w, q, s, n, col, r):
                dve.wait_ge(score_full, l * WL + w + 1)
                dve.tensor_reduce(rmax[0:n, s:s + 1], score[0:n, :, 0:HALF], AX.XY, ALU.max).then_inc(max_ready, 1)
                dve.wait_ge(rs_ready, l * RL + r + 2)
                dve.wait_ge(max_ready, l * QTL + q + 1)
                dve.tensor_scalar(nbias[0:n, s:s + 1], rmax[0:n, s:s + 1], rs[0:n, col:col + 1], -1.0,
                                  ALU.mult, ALU.mult).then_inc(bias_ready, 1)

            def normalise(l, w, q, s, n):
                dve.wait_ge(score_free, l * WL + w + 2)
                dve.reciprocal(rinv[0:n, s:s + 1], rsum[0:n, s:s + 1]).then_inc(rinv_ready, 1)
                dve.wait_ge(rinv_ready, l * QTL + q + 1)
                dve.tensor_scalar(prob[0:n, s, :], prob[0:n, s, :], rinv[0:n, s:s + 1], None, ALU.mult
                                  ).then_inc(prob_ready, 1)

            def probs_lo(l, q, n, at):
                dve.wait_ge(pt_hi_ready, l * QTL + q + 1)
                dve.tensor_tensor(pt_lo[:, :, at:at + n], turn[:, 0:4 * n].rearrange("p (c q) -> p c q", c=4),
                                  pt_hi[:, :, at:at + n].bitcast(F32), ALU.subtract).then_inc(turn_free, 1)

            def tail_lo_part(l, n_tail, n):
                dve.wait_ge(tail_hi_ready, l * ATT + n_tail + 1)
                dve.tensor_tensor(tail_lo[0:META, 0:n], mixed[0:META, 0:n], tail_hi[0:META, 0:n].bitcast(F32),
                                  ALU.subtract).then_inc(mixed_free, 1)

            def silus(l, T, h):
                dve.wait_ge(tile_taken, l * TL + T + 3)
                dve.wait_ge(tanh_ready, l * HL + h + 1)
                dve.scalar_tensor_tensor(agm[:, h, :], ag_th[:, 0:META], 1.0, ag_raw[:, 0:META], ALU.add, ALU.mult)
                dve.scalar_tensor_tensor(silu, ag_th, 1.0, ag_raw, ALU.add, ALU.mult).then_inc(silu_ready, 1)

            def output(l, n, o, dst, src, gate):
                dve.wait_ge(att_done, l * ATT + n + 1)
                dve.wait_ge(mixed_full, l * OL + o + 1)
                dve.scalar_tensor_tensor(dst, src, 0.5, gate, ALU.mult, ALU.mult).then_inc(mixed_free, 1)

            def head(l, h, last=False):
                w, o, q = W_HEAD + 4 * h, O_HEAD + 2 * h, 4 * h
                A, B, r = T_HEAD + 2 * h, T_HEAD + 1 + 2 * h, R_Q0 + h
                maximum(l, w, q, 0, P, Q_COL, r)
                normalise(l, w, q, 0, P)
                maximum(l, w + 1, q + 1, 1, P, Q_COL + 1, r)
                probs_lo(l, q, P, 0)
                normalise(l, w + 1, q + 1, 1, P)
                split_lo(l, B, odd=0)
                maximum(l, w + 2, q + 2, 0, P, Q_COL + 2, r)
                probs_lo(l, q + 1, P, P)
                normalise(l, w + 2, q + 2, 0, P)
                if last:
                    take(l, A, fgate[:, 0, :], odd=1)
                else:
                    take_rope(l, A, 3 + h, odd=1)
                maximum(l, w + 3, q + 3, 1, P, Q_COL + 3, r)
                probs_lo(l, q + 2, P, 2 * P)
                normalise(l, w + 3, q + 3, 1, P)
                if not last:
                    rotate_cos(l, 3 + h, 0, A, split=3 + h)
                tail_lo_part(l, h, 4 * P)
                probs_lo(l, q + 3, P, 3 * P)
                if not last:
                    rotate_sin(l, 3 + h, 0, l * (ROPES - 1) + h + 2)
                take(l, B, ag_raw, odd=0)
                if last:
                    mean_squares(l, U_HEAD + 5 * h + 4, R_QM, 4 * META, M_COL, KV, 1.0, HD * EPS)
                else:
                    mean_squares(l, U_HEAD + 5 * h + 4, r + 1, P, Q_COL, ROW_TILES, 1.0, HD * EPS)
                split_lo(l, A + 2, odd=1)
                silus(l, B, h)
                dve.wait_ge(silu_ready, l * HEADS + h + 1)
                output(l, h, o + 1, att[:, META:S], mixed[:, :], silu[:, META:S])

            def meta_probs_lo(l, kv):
                probs_lo(l, QT_M0 + kv, 4 * META, 0)
                tail_lo_part(l, A_M0 + kv, 4 * META)

            def meta_output(l, kv):
                output(l, A_M0 + kv, O_M0 + 2 * kv + 1, att[:, 0:4 * META], mixed[:, 0:4 * META],
                       flat(agm[:, 4 * kv:4 * kv + 4, :]))

            def fourier_gate(l, T, g):
                dve.wait_ge(tile_taken, l * TL + T + 3)
                dve.wait_ge(tanh_ready, l * HL + H_FG + g + 1)
                dve.scalar_tensor_tensor(fgate[:, g, :], ag_th, 1.0, fgate[:, g, :], ALU.add, ALU.mult
                                         ).then_inc(fgate_ready, 1)

            def table_lo(l, n, dst, src, hi, freed):
                dve.wait_ge(ft_hi_ready, l * 3 + n + 1)
                dve.tensor_tensor(dst, src, hi.bitcast(F32), ALU.subtract).then_inc(freed, 1)

            def fold_group(l, g, T):
                take(l, T, fv, odd=1)
                dve.wait_ge(tile_taken, l * TL + T + 3)
                dve.wait_ge(fold_ready, l * FG + g + 1)
                dve.tensor_copy(fold[:, 0, 0:FOLD + 1:FOLD], fv[:, 0:FOLD + 1:FOLD])
                dve.tensor_tensor(fold[:, 0, 1:FOLD], fv[:, 1:FOLD], fv[:, S - 1:FOLD:-1], ALU.add)
                dve.tensor_tensor(fold[:, 1, 1:FOLD], fv[:, 1:FOLD], fv[:, S - 1:FOLD:-1],
                                  ALU.subtract).then_inc(folded, 1)

            def channels_lo_part(l, g):
                dve.wait_ge(pq_hi_ready, l * FG + g + 1)
                dve.tensor_tensor(pq_lo[0:FT].rearrange("p (a c) n -> p a (c n)", a=2), score[0:FT, :, 0:FCH * P],
                                  pq_hi[0:FT].rearrange("p (a c) n -> p a (c n)", a=2).bitcast(F32),
                                  ALU.subtract).then_inc(score_free, 1)

            def unfold(l, g):
                dve.wait_ge(z_ready, l * FG + g + 1)
                dve.wait_ge(turn_full, l * UL + U_A + g + 1)
                dve.wait_ge(mixed_free, l * OL + O_B + g + 2)
                dve.tensor_tensor(fz[:, 0:FOLD + 1], turn[:, 0:FOLD + 1], fb[:, 0:FOLD + 1], ALU.subtract)
                dve.tensor_tensor(fz[:, S - 1:FOLD:-1], turn[:, 1:FOLD], fb[:, 1:FOLD], ALU.add).then_inc(turn_free, 1)
                dve.wait_ge(turn_free, l * UL + U_A + g + 2)
                dve.wait_ge(fgate_ready, l * FG + g + 1)
                dve.scalar_tensor_tensor(fz, fz, 0.5, fgate[:, g, :], ALU.mult, ALU.mult).then_inc(z_gated, 1)

            def gated(l, j, b):
                T = T_MIX + 4 * j
                g, y = (gf, yf) if b else (ga, ya)
                dve.wait_ge(m_ready, l * NC + j + 1)
                dve.wait_ge(tanh_ready, l * HL + H_MIX + 2 * j + 2)
                dve.wait_ge(tile_done, l * TL + T + b + 5)
                dve.scalar_tensor_tensor(halves(y), halves(g), 1.0, result(b), ALU.add, ALU.mult
                                         ).then_inc(tile_taken, 1)
                split_lo(l, T + 4 + b, odd=b)

            for s, n in ((w_ready, 2), (tile_taken, 2), (turn_free, 1), (score_free, 1), (mixed_free, 1)):
                dve.sem_inc(s, n)
            dve.memset(ones[:], 1.0).then_inc(const_ready, 1)
            dve.memset(halfneg[:], -0.5).then_inc(const_ready, 1)
            dve.memset(ngain[:, DEPTH, :], 0.0).then_inc(const_ready, 1)
            def init_sums(c):
                dve.wait_ge(hsq_ready, c + 1)
                if c == 0:
                    dve.tensor_copy(sqsum[:], hsq[:, 0, :]).then_inc(hsq_added, 1)
                else:
                    dve.wait_ge(hsq_added, c + 2)
                    dve.tensor_tensor(sqsum[:], sqsum[:], hsq[:, c % 2, :], ALU.add).then_inc(hsq_added, 1)

            dve.wait_ge(gain_in, 16)
            for c in range(NC):
                main, rest = (score[:, 0, :], score[:, 1, :]) if c % 2 == 0 else (turn, mixed)
                dve.wait_ge(x_turned, c + 1)
                dve.tensor_copy(h_t[:, c, 0:META], rest[:, 0:META]).then_inc(h_ready, 1)
                if c % 2 == 0:
                    dve.tensor_copy(h_t[:, c, META:S], main[:, 0:SEQ]).then_inc(h_ready, 1)
                else:
                    dve.wait_ge(h_ready_odd, c // 2 + 1)
                dve.wait_ge(h_ready, by_dve(c))
                absorb(c, 0, c, c % 2)
                if c:
                    init_sums(c - 1)
                if c == 4:
                    split_lo(0, T_K0)
            init_sums(NC - 1)
            split_lo(0, T_K1)
            dve.wait_ge(param_in, 16 * PARAMS)
            dve.wait_ge(bias_in, 16)
            dve.tensor_scalar(bhalf[:], bhalf[:], 0.5, None, ALU.mult).then_inc(const_ready, 1)

            with dve.Fori(0, DEPTH) as l:
                mean_squares(l, U_RMS, R_H, NT, 0, NP_, 1.0 / D, EPS)
                diagonals(l, R_H, 0)
                split_lo(l, T_Q0)
                dve.wait_ge(score_full, l * WL + W_RMS + 1)
                dve.tensor_copy(halves(rstd[:]), score[:, :, 0:HALF]).then_inc(score_free, 1)
                dve.wait_ge(score_free, l * WL + W_RMS + 2)
                take_rope(l, T_K0, 0)
                dve.wait_ge(rot_loaded, l * 32 + 32)
                for n in range(4):
                    i = dve.tensor_scalar(rot[:, n, :], rot[:, n, :], gains[:, l, n:n + 1], None, ALU.mult)
                i.then_inc(rot_ready, 1)
                take_rope(l, T_K1, 1, rp=1)
                split_lo(l, T_V0)
                dve.wait_ge(rot_ready, l + 1)
                rotate(l, 0, 2, l * (ROPES - 1), T_K0, split=0)
                mean_squares(l, U_K0, R_K0, NT, 0, NP_, 1.0 / HD, EPS)
                rotate(l, 1, 2, l, T_K1, rp=1)
                diagonals(l, R_K0, 1)
                take_rope(l, T_Q0, 2)
                split_lo(l, T_V1)
                mean_squares(l, U_K1, R_K1, NT, 0, NP_, 1.0 / HD, EPS)
                scale_k(l, 0)
                diagonals(l, R_K1, 2)
                rotate(l, 2, 0, l * (ROPES - 1) + 1, T_Q0, split=1)
                scale_k(l, 1)
                take(l, T_V0, v_t[:, 0, :])
                split_lo(l, T_HEAD)
                value_lo(l, 0)
                take(l, T_V1, v_t[:, 1, :])
                mean_squares(l, U_Q0, R_Q0, P, Q_COL, ROW_TILES, 1.0, HD * EPS)
                value_lo(l, 1)
                with dve.Fori(0, HEADS - 1) as h:
                    head(l, h)
                head(l, HEADS - 1, True)
                maximum(l, W_M0, QT_M0, 0, 4 * META, M_COL, R_QM)
                split_lo(l, T_FOUR + 1)
                normalise(l, W_M0, QT_M0, 0, 4 * META)
                maximum(l, W_M0 + 1, QT_M0 + 1, 1, 4 * META, M_COL + 1, R_QM)
                meta_probs_lo(l, 0)
                normalise(l, W_M0 + 1, QT_M0 + 1, 1, 4 * META)
                fourier_gate(l, T_FG0, 0)
                meta_output(l, 0)
                meta_probs_lo(l, 1)
                dve.memset(fold[:, 1, 0:1], 0.0)
                dve.memset(fold[:, :, FOLD:], 0.0).then_inc(fold_zero, 1)
                dve.wait_ge(fold_zero, l + 1)
                fold_group(l, 0, T_FOUR)
                split_lo(l, T_FOUR + 2)
                meta_output(l, 1)
                table_lo(l, 0, cw_lo[:, 0], turn[:, :].rearrange("p (g c) -> p g c", g=FG), cw_hi[:, 0], turn_free)
                table_lo(l, 1, cw_lo[:, 1], mixed[:, :].rearrange("p (g c) -> p g c", g=FG), cw_hi[:, 1], mixed_free)
                table_lo(l, 2, ft_lo[0:FT], ft_raw[0:FT, :].rearrange("p (a b c) -> p a b c", a=2, b=FCH),
                         ft_hi[0:FT], ft_ready)
                take(l, T_FOUR + 1, fgate[:, 1, :])
                channels_lo_part(l, 0)
                split_lo(l, T_FOUR + 3)
                fourier_gate(l, T_FOUR + 1, 1)
                with dve.Fori(1, FG - 1) as g:
                    unfold(l, g - 1)
                    fold_group(l, g, T_FOUR + 2 * g)
                    split_lo(l, T_FOUR + 2 + 2 * g, odd=1)
                    take(l, T_FOUR + 1 + 2 * g, fgate[:, g + 1, :], odd=0)
                    channels_lo_part(l, g)
                    split_lo(l, T_FOUR + 3 + 2 * g, odd=0)
                    fourier_gate(l, T_FOUR + 1 + 2 * g, g + 1)
                unfold(l, FG - 2)
                fold_group(l, FG - 1, T_FOUR + 6)
                split_lo(l, T_MIX + 1)
                take(l, T_MIX, gf)
                split_lo(l, T_MIX + 2)
                channels_lo_part(l, FG - 1)
                unfold(l, FG - 1)
                take(l, T_MIX + 1, ga)
                split_lo(l, T_MIX + 3, n=FG)
                for b in range(2):
                    gated(l, 0, b)
                with dve.Fori(1, NC) as j:
                    T = T_MIX + 4 * j
                    dve.wait_ge(tile_taken, l * TL + T + 2)
                    take(l, T, gf, odd=0)
                    split_lo(l, T + 2, odd=0)
                    take(l, T + 1, ga, odd=1)
                    split_lo(l, T + 3, odd=1, n=FG)
                    for b in range(2):
                        gated(l, j, b)
                with dve.Fori(0, NC // 2) as j:
                    for b in range(2):
                        T, c = T_OUT + 2 * j + b, 2 * j + b
                        dve.wait_ge(tile_done, l * TL + T + 3)
                        dve.scalar_tensor_tensor(halves(h_t[:, c, :]), result(b), 0.5, halves(h_t[:, c, :]),
                                                 ALU.mult, ALU.add).then_inc(tile_taken, 1)
                        dve.wait_ge(tile_taken, l * TL + T + 3)
                        absorb(l * NC + NC + c, l + 1, c, b)
                        split_lo(l, T + 2, odd=b)

            for t in range(ROW_TILES):
                dve.wait_ge(out_turned, 2 * t + 1)
                dve.tensor_copy(by_token[:, t, 0:D // 2], acc[:, t % 2, 0, :]).then_inc(out_ready, 1)

        @block.gpsimd
        def _(pool):
            def minus(dst, a, hi, done):
                pool.tensor_tensor(dst, a, hi.bitcast(F32), ALU.subtract).then_inc(done, 1)

            def x_lo_part(n, c, s):
                pool.wait_ge(xh_ready, n + 1)
                minus(x_lo[:, c, :], xg[:, s, :], x_hi[:, c, :], x_ready)

            def absorb(n, c, s, first):
                x_lo_part(n, c, s)
                wait_apart(pool, hsq_ready, n + 1)
                if first:
                    pool.tensor_copy(sqsum[:], hsq[:, s, :]).then_inc(hsq_added, 1)
                else:
                    pool.wait_ge(hsq_added, n + 2)
                    pool.tensor_tensor(sqsum[:], sqsum[:], hsq[:, s, :], ALU.add).then_inc(hsq_added, 1)

            def power(l, use, rows, at, n, exps_at=None):
                pool.wait_ge(turn_free, l * UL + use + 2)
                if exps_at is not None:
                    pool.wait_ge(score_free, l * WL + exps_at + 2)
                pool.tensor_tensor(rs[0:rows, at:at + n], ms[0:rows, at:at + n], halfneg[0:rows, at:at + n],
                                   ALU.pow).then_inc(rs_ready, 1)

            def k_lo_part(l, kv, n):
                pool.wait_ge(rope_hi, l * ROPES + n + 1)
                minus(k_lo[:, kv, :], ropes[kv][3], k_hi[:, kv, :], rope_done)

            def q_lo_part(l, h, n):
                pool.wait_ge(rope_hi, l * ROPES + n + 1)
                src = ropes[0][2]
                pool.tensor_tensor(qm_lo[:, h, :], src[:, 0:META], qm_hi[:, h, :].bitcast(F32), ALU.subtract)
                minus(q_lo, src, q_hi, rope_done)

            def att_lo_part(l, n):
                pool.wait_ge(att_hi_ready, l * ATT + n + 1)
                minus(place(att_lo, n), made(n), place(att_hi, n), att_done)

            def head(l, h, last=False):
                if last:
                    power(l, U_HEAD + 5 * h + 4, 4 * META, M_COL, KV)
                else:
                    q_lo_part(l, h + 1, 3 + h)
                    power(l, U_HEAD + 5 * h + 4, P, Q_COL, ROW_TILES, W_HEAD + 4 * h + 3)
                att_lo_part(l, h)

            for s, n in ((x_ready, 2), (hsq_added, 2), (rs_ready, 1), (rsq_ready, 1), (rope_ready, 1), (rope_done, 1),
                         (att_done, 1), (fold_ready, 1), (z_ready, 1), (m_ready, 1), (m_done, 1)):
                pool.sem_inc(s, n)
            pool.wait_ge(const_ready, 3)
            pool.dma_start(ngain[:, 0:DEPTH, :], norm_g.rearrange("l (c p) -> p l c", p=P)).then_inc(gain_in, 16)
            pool.dma_start(bhalf[:], b_gate.rearrange("l (c p) -> p l c", p=P)).then_inc(bias_in, 16)
            for c in range(NC):
                x_lo_part(c, c, c % 2)
            with pool.Fori(0, DEPTH) as l:
                power(l, U_RMS, NT, 0, NP_)
                power(l, U_K0, NT, 0, NP_)
                power(l, U_K1, NT, 0, NP_)
                k_lo_part(l, 0, 0)
                q_lo_part(l, 0, 1)
                k_lo_part(l, 1, 2)
                power(l, U_Q0, P, Q_COL, ROW_TILES)
                with pool.Fori(0, HEADS - 1) as h:
                    head(l, h)
                head(l, HEADS - 1, True)
                att_lo_part(l, A_M0)
                att_lo_part(l, A_M0 + 1)
                pool.wait_ge(fold_hi_ready, l * FG + 1)
                minus(xf_lo, fold, xf_hi, fold_ready)
                with pool.Fori(1, FG) as g:
                    pool.wait_ge(z_hi_ready, l * FG + g + 1)
                    minus(z_lo[:, g - 1, :], fz, z_hi[:, g - 1, :], z_ready)
                    pool.wait_ge(fold_hi_ready, l * FG + g + 1)
                    minus(xf_lo, fold, xf_hi, fold_ready)
                pool.wait_ge(z_hi_ready, l * FG + FG + 1)
                minus(z_lo[:, FG - 1, :], fz, z_hi[:, FG - 1, :], z_ready)
                with pool.Fori(0, NC) as j:
                    pool.wait_ge(tile_taken, l * TL + T_MIX + 4 * j + 6)
                    pool.wait_ge(m_done, l * NC + j + 1)
                    pool.tensor_tensor(mm, yf, ya, ALU.add).then_inc(m_ready, 1)
                    pool.wait_ge(m_hi_ready, l * NC + j + 1)
                    minus(m_lo[:, j, :], mm, m_hi[:, j, :], m_done)
                n = l * NC + NC
                absorb(n, 0, 0, True)
                absorb(n + 1, 1, 1, False)
                with pool.Fori(1, NC // 2) as j:
                    for b in range(2):
                        absorb(n + 2 * j + b, 2 * j + b, b, False)


PARAMS = 10


def tables():
    eye = np.eye(P, dtype=np.float32)
    half = HD // 2
    inv = (10000.0 ** (-np.arange(0, half, 2, dtype=np.float32) / np.float32(half))).astype(np.float32)
    t = np.arange(SEQ)
    zero = np.zeros(META, np.float32)
    row = np.concatenate([zero, (t // 64).astype(np.float32)])
    col = np.concatenate([zero, (t % 64).astype(np.float32)])
    ang = [(a[:, None] * inv[None, :]).astype(np.float32).T.astype(np.float64) for a in (row, col)]
    cos = np.concatenate([np.cos(ang[0])] * 2 + [np.cos(ang[1])] * 2)
    sin = np.concatenate([-np.sin(ang[0]), np.sin(ang[0]), -np.sin(ang[1]), np.sin(ang[1])])
    rope = np.stack([cos, sin], axis=1).astype(np.float32)
    tt, ss = np.arange(FT * FCH)[:, None], np.arange(FS)[None, :]
    w = 2 * np.pi * ((tt * ss) % S) / S
    pos = np.stack([np.cos(w), np.sin(w)]).reshape(2, FCH, FT, FS).transpose(2, 0, 1, 3)
    c = np.arange(P)
    v = 2 * np.pi * (np.outer(c, c) % P) / P
    ch = np.concatenate([np.cos(v), np.sin(v)], axis=1) / np.sqrt(S * P)
    return {"eye": eye, "rope": np.ascontiguousarray(rope),
            "dft_pos": np.ascontiguousarray(pos.reshape(FT, 2 * FCH * FS).astype(np.float32)),
            "dft_ch": ch.astype(np.float32)}


INPUTS = ["x", "meta_tokens", "norm_g", "w_in", "b_gate", "q_norm_g", "k_norm_g", "w_fmix", "w_fproj", "w_aproj",
          "w_out"]


def kernel(**inputs):
    import concourse.bacc as bacc
    from concourse.bass_utils import run_bass_kernel_spmd

    nc = bacc.Bacc("TRN2", target_bir_lowering=False, num_devices=1)
    arrays = {"in_" + n: np.ascontiguousarray(inputs[n]) for n in INPUTS}
    arrays.update({"table_" + n: a for n, a in tables().items()})
    args = [nc.dram_tensor(n, a.shape, mybir.dt.from_np(a.dtype), kind="ExternalInput").ap()
            for n, a in arrays.items()]
    out = nc.dram_tensor("out", (1, SEQ, D), F32, kind="ExternalOutput").ap()
    with nc.allow_non_contiguous_dma("gains and biases, a few KB"):
        program(nc, *args, out)
    r = run_bass_kernel_spmd(nc, [arrays], core_ids=[0])
    return r.results[0]["out"]
```
